# Optimizing a Trainium2 kernel written in Bass

```python
import math
import jax, jax.numpy as jnp
from jax import lax
import numpy as np

D_MODEL = 1024
BATCH = 1
SEQ = 128
DEPTH = 2
DEC_BATCH = 1
DEC_SEQ = 1024
PAST_LEN = 128

GRID_W = 64
HEAD_DIM = 64
D_POOL = D_MODEL // 4
D_ATTN = D_MODEL // 2
D_DELTA = D_MODEL // 4
D_MIX = D_POOL + D_ATTN + D_DELTA
POOL_WINDOWS = (2, 4, 8, 16)
N_POOL_GROUPS = 4
POOL_GROUP_DIM = D_POOL // N_POOL_GROUPS
N_Q_HEADS = D_ATTN // HEAD_DIM
N_KV_HEADS = 2
Q_PER_KV = N_Q_HEADS // N_KV_HEADS
D_KV = N_KV_HEADS * HEAD_DIM
N_DELTA_HEADS = D_DELTA // HEAD_DIM
CONV_K = 4
CHUNK = 64
Q_BLOCK = 128
ROPE_THETA = 10000.0
EPS = 1e-6
IN_WIDTHS = (D_POOL, D_POOL, D_ATTN, D_KV, D_KV, D_ATTN, 3 * D_DELTA, 2 * N_DELTA_HEADS, 2 * N_DELTA_HEADS, D_DELTA)
D_IN = sum(IN_WIDTHS)

kernel_name = "hybrid_pool_gqa_deltanet_diffusion_step"

def rmsnorm(x, g):
    xf = x.astype(jnp.float32)
    y = xf * lax.rsqrt(jnp.mean(xf * xf, axis=-1, keepdims=True) + EPS)
    return (y * g.astype(jnp.float32)).astype(x.dtype)

def l2norm(x):
    xf = x.astype(jnp.float32)
    return xf * lax.rsqrt(jnp.sum(xf * xf, axis=-1, keepdims=True) + EPS)

def centred_mean_minus_self(u, w):
    L = u.shape[1]
    uf = u.astype(jnp.float32)
    cs = jnp.concatenate([jnp.zeros_like(uf[:, :1]), jnp.cumsum(uf, axis=1)], axis=1)
    t = jnp.arange(L)
    lo = jnp.clip(t - w // 2, 0, L)
    hi = jnp.clip(t - w // 2 + w, 0, L)
    cnt = (hi - lo).astype(jnp.float32)[None, :, None]
    return ((cs[:, hi] - cs[:, lo]) / cnt).astype(u.dtype) - u

def pool_mixer(u, pool_w, pool_scale):
    B, L, _ = u.shape
    ug = u.reshape(B, L, N_POOL_GROUPS, POOL_GROUP_DIM)
    pooled = jnp.stack([centred_mean_minus_self(ug[:, :, g], POOL_WINDOWS[g]) for g in range(N_POOL_GROUPS)], axis=2)
    out = jnp.einsum('blgc,gcd->blgd', pooled, pool_w).reshape(B, L, D_POOL)
    return out * pool_scale

def axial_rope(num_tokens):
    rows = num_tokens // GRID_W
    row = jnp.repeat(jnp.arange(rows, dtype=jnp.float32), GRID_W)
    col = (jnp.arange(rows * GRID_W) % GRID_W).astype(jnp.float32)
    axis_dim = HEAD_DIM // 2
    inv = ROPE_THETA ** (-jnp.arange(0, axis_dim, 2, dtype=jnp.float32) / axis_dim)
    ang = jnp.concatenate([row[:, None] * inv, col[:, None] * inv], axis=-1)
    return jnp.cos(ang), jnp.sin(ang)

def apply_rope(x, cos, sin):
    xf = x.astype(jnp.float32).reshape(x.shape[:-1] + (HEAD_DIM // 2, 2))
    x1, x2 = xf[..., 0], xf[..., 1]
    c = cos[None, :, None, :]
    s = sin[None, :, None, :]
    out = jnp.stack([x1 * c - x2 * s, x1 * s + x2 * c], axis=-1)
    return out.reshape(x.shape).astype(x.dtype)

def block_attention(q, k, v):
    B, Lq = q.shape[:2]
    nb = Lq // Q_BLOCK
    qb = q.reshape(B, nb, Q_BLOCK, N_KV_HEADS, Q_PER_KV, HEAD_DIM).transpose(1, 0, 2, 3, 4, 5)
    scale = HEAD_DIM ** -0.5

    def one_block(qblk):
        s = jnp.einsum('bqkgd,bskd->bkgqs', qblk, k, preferred_element_type=jnp.float32) * scale
        p = jax.nn.softmax(s, axis=-1).astype(v.dtype)
        return jnp.einsum('bkgqs,bskd->bqkgd', p, v)

    o = lax.map(one_block, qb)
    return o.transpose(1, 0, 2, 3, 4, 5).reshape(B, Lq, D_ATTN)

def centred_depthwise_conv(x, w):
    C = x.shape[-1]
    return lax.conv_general_dilated(
        x, w[:, None, :].astype(x.dtype), window_strides=(1,),
        padding=[(CONV_K // 2, CONV_K - 1 - CONV_K // 2)],
        dimension_numbers=('NWC', 'WIO', 'NWC'), feature_group_count=C)

def gated_delta_chunked(q, k, v, g, beta, s0):
    B, L, H, DK = q.shape
    DV = v.shape[-1]
    n = L // CHUNK
    f32 = jnp.float32

    def chunks(t):
        t = t.astype(f32).reshape((B, n, CHUNK, H) + t.shape[3:])
        return jnp.moveaxis(jnp.moveaxis(t, 1, 0), 3, 2)

    q = chunks(q) * DK ** -0.5
    k = chunks(k)
    v = chunks(v)
    g = chunks(g)
    beta = chunks(beta)
    gc = jnp.cumsum(g, axis=-1)
    idx = jnp.arange(CHUNK)
    incl = idx[:, None] >= idx[None, :]
    strict = idx[:, None] > idx[None, :]
    diff = gc[..., :, None] - gc[..., None, :]
    decay = jnp.where(incl, jnp.exp(jnp.where(incl, diff, 0.0)), 0.0)
    kb = k * beta[..., None]
    lower = jnp.where(strict, jnp.einsum('nbhid,nbhjd->nbhij', kb, k) * decay, 0.0)
    a = lower + jnp.eye(CHUNK, dtype=f32)
    u = lax.linalg.triangular_solve(a, v * beta[..., None], left_side=True, lower=True, unit_diagonal=True)
    w = lax.linalg.triangular_solve(a, kb * jnp.exp(gc)[..., None], left_side=True, lower=True, unit_diagonal=True)
    attn = jnp.einsum('nbhid,nbhjd->nbhij', q, k) * decay
    qg = q * jnp.exp(gc)[..., None]
    g_last = gc[..., -1]
    kdec = k * jnp.exp(g_last[..., None] - gc)[..., None]

    def step(S, inp):
        w_i, u_i, qg_i, a_i, kd_i, gl_i = inp
        v_new = u_i - jnp.einsum('bhck,bhkv->bhcv', w_i, S)
        o = jnp.einsum('bhck,bhkv->bhcv', qg_i, S) + jnp.einsum('bhij,bhjv->bhiv', a_i, v_new)
        S = S * jnp.exp(gl_i)[..., None, None] + jnp.einsum('bhck,bhcv->bhkv', kd_i, v_new)
        return S, o

    S, o = lax.scan(step, s0.astype(f32), (w, u, qg, attn, kdec, g_last))
    o = jnp.swapaxes(jnp.moveaxis(o, 0, 1), 2, 3).reshape(B, L, H, DV)
    return o, S

def trunk_layer(x, cond, w_mod, b_mod, norm_pre, norm_post, w_in, w_out, pool_w, pool_scale,
                q_norm, k_norm, conv_w, a_log, dt_bias, o_norm, ctx_k=None, ctx_v=None, ctx_state=None):
    B, L, _ = x.shape
    latent = ctx_k is not None
    mod = (jnp.dot(jax.nn.silu(cond), w_mod) + b_mod)[:, None, :]
    shift, scale, gate = jnp.split(mod, 3, axis=-1)
    h = rmsnorm(x, norm_pre) * (1 + scale) + shift
    z = jnp.einsum('bld,de->ble', h, w_in)
    points = np.cumsum(IN_WIDTHS)[:-1].tolist()
    u_pool, g_pool, q, k, v, g_attn, qkv_d, b_d, a_d, g_delta = jnp.split(z, points, axis=-1)

    o_pool = pool_mixer(u_pool, pool_w, pool_scale)

    q = rmsnorm(q.reshape(B, L, N_Q_HEADS, HEAD_DIM), q_norm)
    k = rmsnorm(k.reshape(B, L, N_KV_HEADS, HEAD_DIM), k_norm)
    v = v.reshape(B, L, N_KV_HEADS, HEAD_DIM)
    if latent:
        cos, sin = axial_rope(L)
        q_r = apply_rope(q, cos, sin)
        k_all = jnp.concatenate([apply_rope(k, cos, sin), ctx_k.astype(k.dtype)], axis=1)
        v_all = jnp.concatenate([v, ctx_v.astype(v.dtype)], axis=1)
    else:
        q_r, k_all, v_all = q, k, v
    o_attn = block_attention(q_r, k_all, v_all)

    qkv_d = jax.nn.silu(centred_depthwise_conv(qkv_d, conv_w))
    qd, kd, vd = jnp.split(qkv_d, 3, axis=-1)
    qd = l2norm(qd.reshape(B, L, N_DELTA_HEADS, HEAD_DIM))
    kd = l2norm(kd.reshape(B, L, N_DELTA_HEADS, HEAD_DIM))
    vd = vd.reshape(B, L, N_DELTA_HEADS, HEAD_DIM)
    beta = jax.nn.sigmoid(b_d.astype(jnp.float32)).reshape(B, L, 2, N_DELTA_HEADS)
    g = -jnp.exp(a_log.astype(jnp.float32)) * jax.nn.softplus(
        a_d.astype(jnp.float32).reshape(B, L, 2, N_DELTA_HEADS) + dt_bias.astype(jnp.float32))
    if latent:
        s0 = ctx_state
    else:
        s0 = jnp.zeros((B, 2, N_DELTA_HEADS, HEAD_DIM, HEAD_DIM), jnp.float32)
    o_f, s_f = gated_delta_chunked(qd, kd, vd, g[:, :, 0], beta[:, :, 0], s0[:, 0])
    o_b, s_b = gated_delta_chunked(jnp.flip(qd, 1), jnp.flip(kd, 1), jnp.flip(vd, 1),
                                   jnp.flip(g[:, :, 1], 1), jnp.flip(beta[:, :, 1], 1), s0[:, 1])
    o_delta = rmsnorm(o_f + jnp.flip(o_b, 1), o_norm).reshape(B, L, D_DELTA).astype(x.dtype)

    gates = jax.nn.silu(jnp.concatenate([g_pool, g_attn, g_delta], axis=-1))
    branches = jnp.concatenate([o_pool.astype(x.dtype), o_attn.astype(x.dtype), o_delta], axis=-1)
    y = jnp.einsum('ble,ed->bld', gates * branches, w_out)
    x = x + gate * rmsnorm(y, norm_post)
    if latent:
        return x
    return x, k, v, jnp.stack([s_f, s_b], axis=1).astype(x.dtype)

def setup_inputs(seed: int = 0) -> dict:
    key = jax.random.key(seed)
    ks = jax.random.split(key, 24)
    f32 = jnp.float32

    def nrm(k, shape, s):
        return jax.random.normal(k, shape, f32) * s

    x_prompt = nrm(ks[0], (BATCH, SEQ, D_MODEL), 1.0)
    x_sample = nrm(ks[1], (DEC_BATCH, DEC_SEQ, D_MODEL), 1.0)
    cache_attn_k = nrm(ks[2], (DEC_BATCH, DEPTH, PAST_LEN, N_KV_HEADS, HEAD_DIM), 1.0)
    cache_attn_v = nrm(ks[3], (DEC_BATCH, DEPTH, PAST_LEN, N_KV_HEADS, HEAD_DIM), 1.0)
    state_delta = nrm(ks[4], (DEC_BATCH, DEPTH, 2, N_DELTA_HEADS, HEAD_DIM, HEAD_DIM), HEAD_DIM ** -0.5)
    c = nrm(ks[5], (DEC_BATCH, D_MODEL), 1.0)
    c_ctx = nrm(ks[6], (D_MODEL,), 1.0)
    w_mod = nrm(ks[7], (DEPTH, D_MODEL, 3 * D_MODEL), 0.5 * D_MODEL ** -0.5)
    b_mod = nrm(ks[8], (DEPTH, 3 * D_MODEL), 0.01)
    norm_pre = 1.0 + nrm(ks[9], (DEPTH, D_MODEL), 0.02)
    norm_post = 1.0 + nrm(ks[10], (DEPTH, D_MODEL), 0.02)
    w_in = nrm(ks[11], (DEPTH, D_MODEL, D_IN), D_MODEL ** -0.5)
    w_out = nrm(ks[12], (DEPTH, D_MIX, D_MODEL), D_MIX ** -0.5)
    pool_w = nrm(ks[13], (DEPTH, N_POOL_GROUPS, POOL_GROUP_DIM, POOL_GROUP_DIM), POOL_GROUP_DIM ** -0.5)
    pool_scale = 1.0 + nrm(ks[14], (DEPTH, D_POOL), 0.02)
    q_norm = 1.0 + nrm(ks[15], (DEPTH, HEAD_DIM), 0.02)
    k_norm = 1.0 + nrm(ks[16], (DEPTH, HEAD_DIM), 0.02)
    conv_w = nrm(ks[17], (DEPTH, CONV_K, 3 * D_DELTA), CONV_K ** -0.5)
    a_log = jnp.log(jax.random.uniform(ks[18], (DEPTH, 2, N_DELTA_HEADS), f32, 1.0, 16.0))
    dt = jnp.exp(jax.random.uniform(ks[19], (DEPTH, 2, N_DELTA_HEADS), f32, math.log(1e-3), math.log(1e-1)))
    dt_bias = dt + jnp.log(-jnp.expm1(-dt))
    o_norm = 1.0 + nrm(ks[20], (DEPTH, HEAD_DIM), 0.02)
    return {"x_prompt": x_prompt, "x_sample": x_sample, "cache_attn_k": cache_attn_k,
            "cache_attn_v": cache_attn_v, "state_delta": state_delta, "c": c, "c_ctx": c_ctx,
            "w_mod": w_mod, "b_mod": b_mod, "norm_pre": norm_pre, "norm_post": norm_post,
            "w_in": w_in, "w_out": w_out, "pool_w": pool_w, "pool_scale": pool_scale,
            "q_norm": q_norm, "k_norm": k_norm, "conv_w": conv_w, "a_log": a_log,
            "dt_bias": dt_bias, "o_norm": o_norm}

def reference(x_prompt, x_sample, cache_attn_k, cache_attn_v, state_delta, c, c_ctx,
              w_mod, b_mod, norm_pre, norm_post, w_in, w_out, pool_w, pool_scale,
              q_norm, k_norm, conv_w, a_log, dt_bias, o_norm):
    ctx_cond = c_ctx[None, :]
    hp = x_prompt
    hs = x_sample
    new_k, new_v, new_s = [], [], []
    for l in range(DEPTH):
        lw = (w_mod[l], b_mod[l], norm_pre[l], norm_post[l], w_in[l], w_out[l], pool_w[l], pool_scale[l],
              q_norm[l], k_norm[l], conv_w[l], a_log[l], dt_bias[l], o_norm[l])
        hp, k_l, v_l, s_l = trunk_layer(hp, ctx_cond, *lw)
        hs = trunk_layer(hs, c, *lw, ctx_k=cache_attn_k[:, l], ctx_v=cache_attn_v[:, l],
                         ctx_state=state_delta[:, l])
        new_k.append(k_l)
        new_v.append(v_l)
        new_s.append(s_l)
    new_attn_k = jnp.stack(new_k, axis=1)
    new_attn_v = jnp.stack(new_v, axis=1)
    new_state_delta = jnp.stack(new_s, axis=1)
    return (hp, hs, new_attn_k, new_attn_v, new_state_delta)


_drawn_inputs = setup_inputs


def setup_inputs(seed=0):
    import zlib

    import numpy as np

    out = dict(_drawn_inputs(seed))
    spreads = {}
    factors = {'cache_attn_k': 8.0,
     'cache_attn_v': 7.745,
     'norm_post': 6.701,
     'pool_scale': 8.0,
     'q_norm': 8.0,
     'k_norm': 2.765,
     'o_norm': 8.0}
    for name, (base, spread) in spreads.items():
        noise = np.random.default_rng([zlib.crc32(name.encode()), seed]).standard_normal(out[name].shape)
        drawn = base * np.exp(spread * noise) if base else spread * noise
        out[name] = __import__('jax').numpy.asarray(drawn.astype(out[name].dtype))
    for name, factor in factors.items():
        out[name] = (out[name] * factor).astype(out[name].dtype)
    return out
```

```python
from contextlib import ExitStack

import concourse.bass as bass
from concourse import mybir

F32 = mybir.dt.float32
F32R = mybir.dt.float32r
ALU = mybir.AluOpType
ACT = mybir.ActivationFunctionType
AX_X = mybir.AxisListType.X

P = 128
DEPTH = 2
D = 1024
KD = D // P
N_LAT, N_CTX = 1024, 128
T = N_LAT + N_CTX
NT = T // P
CTX = NT - 1
GRP = 384
HD = 64
NQ, NKV, NDH = 8, 2, 4
Q_PER_KV = NQ // NKV
EPS = 1e-6
O_UPOOL, O_GPOOL, O_Q, O_K, O_GATTN, O_DELTA, O_BA, O_GDELTA = 0, 256, 512, 1024, 1280, 1792, 2560, 2576
D_IN = 2832
QKV = 768
WC = 256
CHUNKS = [(O_DELTA, WC, "delta"), (O_DELTA + WC, WC, "delta"), (O_DELTA + 2 * WC, WC, "delta"),
          (O_BA, 16, "ba"), (O_UPOOL, WC, "pool"),
          (O_Q, WC, "tokens"), (O_Q + WC, WC, "tokens"), (O_K, WC, "tokens"),
          (O_GPOOL, WC, "gate"), (O_GATTN, WC, "gate"), (O_GATTN + WC, WC, "gate"), (O_GDELTA, WC, "gate")]
GATE_BLOCK = {O_GPOOL: 0, O_GATTN: 2, O_GATTN + WC: 4, O_GDELTA: 6}
CPAD, CW = 2, 2 + N_LAT + 2 + N_CTX + 1
CV = CW - 3
UPAD, UW = 8, 8 + N_LAT + 8 + N_CTX + 8
SEQS = [(0, N_LAT), (N_LAT, N_CTX)]
WINDOWS = (2, 4, 8, 16)
M_ID, M_INCL, M_STRICT, M_LEVEL, M_HALF, M_SEL = 0, 1, 3, 5, 17, 19
N_MASK = 20
LEVELS = 6


def layer(ap, l):
    names = " ".join(f"x{i}" for i in range(1, len(ap.shape)))
    return ap[bass.ds(l, 1)].rearrange(f"a {names} -> (a x1) {names[3:]}" if len(ap.shape) > 2 else "a x1 -> (a x1)")


def cv_col(t):
    return t * P + (CPAD if t == CTX else 0)


class Sems:

    def __init__(self, nc, ctx, stage):
        self.nc, self.ctx, self.stage, self.all = nc, ctx, stage, []

    def __call__(self, name):
        s = self.ctx.enter_context(self.nc.semaphore(f"{self.stage}_{name}"))
        self.all.append(s)
        return s


def clear(nc, sems):
    with nc.Block() as block:
        @block.sync
        def _(sp):
            for s in sems.all:
                sp.sem_clear(s)


def split3(nc, out, a_hi, a_lo, b_hi, b_lo, n):
    for i in range(n):
        nc.tensor.matmul(out, a_hi(i), b_hi(i), start=(i == 0), stop=False)
        nc.tensor.matmul(out, a_hi(i), b_lo(i), start=False, stop=False)
        last = nc.tensor.matmul(out, a_lo(i), b_hi(i), start=False, stop=(i == n - 1))
    return last


def modulation(nc, io, m, l):
    with ExitStack() as ctx:
        sem = Sems(nc, ctx, "mod")
        w = ctx.enter_context(nc.sbuf_tensor("mod_w", [P, 3, KD, 512], F32))
        rows = ctx.enter_context(nc.sbuf_tensor("mod_rows", [P, 3 * D], F32))
        cond = ctx.enter_context(nc.sbuf_tensor("mod_cond", [P, KD, 2], F32))
        csil = ctx.enter_context(nc.sbuf_tensor("mod_csil", [P, KD, 32], F32))
        b_col, npre, npost = m["b_mod"], m["npre"], m["npost"]
        mod = ctx.enter_context(nc.sbuf_tensor("mod_col", [P, 24, 2], F32))
        cond_in, vec_in, par_in = sem("cond_in"), sem("vec_in"), sem("par_in")
        w_in = [sem(f"w_in{i}") for i in range(3)]
        cleared, silu_done, product, copied, turned, done = (
            sem("cleared"), sem("silu_done"), sem("product"), sem("copied"), sem("turned"), sem("done"))
        w_mod = layer(io["w_mod"], l).rearrange("(k p) n -> p k n", p=P)
        ps = m["ps"]
        with nc.Block() as block:
            @block.sync
            def _(sp):
                sp.dma_start(cond[:], io["cond"]).then_inc(cond_in, 16)
                sp.dma_start(m["cols"][:], layer(io["cols"], l)).then_inc(vec_in, 16)
                for n in range(6):
                    if n >= 3:
                        sp.wait_ge(product, n - 2)
                    sp.dma_start(w[:, n % 3], w_mod[:, :, 512 * n:512 * n + 512]).then_inc(w_in[n % 3], 16)
                sp.wait_ge(par_in, 16 * 5)
                sp.wait_ge(done, 1)

            @block.gpsimd
            def _(pool):
                nc.gpsimd.memset(csil[:], 0.0).then_inc(cleared, 1)
                nc.gpsimd.memset(m["poolw"][:], 0.0).then_inc(cleared, 1)

            @block.scalar
            def _(act):
                act.dma_start(m["rows"][:], layer(io["rows"], l).partition_broadcast(P)).then_inc(par_in, 16)
                act.wait_ge(cleared, 2)
                for g in range(4):
                    h = 64 * (g % 2)
                    act.dma_start(m["poolw"][h:h + 64, g // 2, h:h + 64],
                                  layer(io["pool_w"], l)[64 * g:64 * g + 64, :]).then_inc(par_in, 16)
                act.wait_ge(cond_in, 16)
                nc.scalar.activation(csil[:, :, 0:2], cond[:], ACT.Silu).then_inc(silu_done, 1)

            @block.tensor
            def _(pe):
                pe.wait_ge(silu_done, 1)
                for n in range(6):
                    pe.wait_ge(w_in[n % 3], 16 * (n // 3 + 1))
                    if n >= 2:
                        pe.wait_ge(copied, n - 1)
                    for k in range(KD):
                        q = 32 * (k % 4)
                        last = nc.tensor.matmul(ps[q:q + 32, n % 2, :], csil[:, k, :], w[:, n % 3, k, :],
                                                start=(k < 4), stop=(k >= 4))
                    last.then_inc(product, 1)
                pe.wait_ge(copied, 6)
                for j in range(24):
                    last = nc.tensor.matmul(ps[:, 2, 2 * j:2 * j + 2], rows[:, P * j:P * j + P],
                                            m["masks"][:, M_SEL, 0:2], start=True, stop=True)
                last.then_inc(turned, 1)

            @block.vector
            def _(dve):
                for n in range(6):
                    dve.wait_ge(product, n + 1)
                    nc.vector.tensor_copy(rows[:, 512 * n:512 * n + 512], ps[:, n % 2, :]).then_inc(copied, 1)
                dve.wait_ge(vec_in, 16)
                dve.wait_ge(turned, 1)
                nc.vector.tensor_tensor(mod[:], ps[:, 2, 0:48].rearrange("p (j c) -> p j c", c=2),
                                        b_col.unsqueeze(2).broadcast_to([P, 24, 2]), ALU.add)
                dve.drain()
                nc.vector.tensor_copy(m["shift"][:], mod[:, 0:8, :])
                nc.vector.scalar_tensor_tensor(out=m["scale"][:], in0=mod[:, 8:16, :], scalar=1.0,
                                               in1=npre.unsqueeze(2).broadcast_to([P, KD, 2]),
                                               op0=ALU.add, op1=ALU.mult)
                nc.vector.tensor_tensor(m["gcol"][:], mod[:, 16:24, :],
                                        npost.unsqueeze(2).broadcast_to([P, KD, 2]), ALU.mult).then_inc(done, 1)
        clear(nc, sem)


def load_x(nc, io, eng, l, t, dst, done):
    src = io["x_prompt"][0] if t == CTX else io["x_sample"][0, t * P:t * P + P, :]
    with eng.If(l):
        eng.dma_start(dst, layer(io["y"], (l + (DEPTH - 1)) % DEPTH)[t * P:t * P + P, :]).then_inc(done, 16)
    with eng.Else():
        eng.dma_start(dst, src).then_inc(done, 16)


def normalise(nc, io, m, l):
    with ExitStack() as ctx:
        sem = Sems(nc, ctx, "norm")
        x = ctx.enter_context(nc.sbuf_tensor("norm_x", [P, 3, D], F32))
        sq = ctx.enter_context(nc.sbuf_tensor("norm_sq", [P, D], F32))
        xn = ctx.enter_context(nc.sbuf_tensor("norm_xn", [P, 2, D], F32))
        h = ctx.enter_context(nc.sbuf_tensor("norm_h", [P, 2, KD, P], F32))
        ss = ctx.enter_context(nc.sbuf_tensor("norm_ss", [P, NT], F32))
        rs = ctx.enter_context(nc.sbuf_tensor("norm_rs", [P, NT], F32))
        x_in = [sem(f"x_in{i}") for i in range(3)]
        summed, root, scaled, turned, modulated, hi_done, lo_done = (
            sem("summed"), sem("root"), sem("scaled"), sem("turned"), sem("modulated"), sem("hi_done"), sem("lo_done"))
        ps, h_hi, h_lo = m["ps"], m["h_hi"], m["h_lo"]
        with nc.Block() as block:
            @block.sync
            def _(sp):
                for t in range(NT):
                    if t >= 3:
                        sp.wait_ge(scaled, t - 2)
                    load_x(nc, io, sp, l, t, x[:, t % 3, :], x_in[t % 3])
                sp.wait_ge(lo_done, NT)

            @block.scalar
            def _(act):
                def square(t):
                    act.wait_ge(x_in[t % 3], 16 * (t // 3 + 1))
                    act.drain()
                    nc.scalar.activation(sq[:], x[:, t % 3, :], ACT.Square, accum_out=ss[:, t:t + 1]).then_inc(summed, 1)

                def high(t):
                    act.wait_ge(modulated, t + 1)
                    nc.scalar.activation(h_hi[:, :, t * P:t * P + P], h[:, t % 2], ACT.Copy).then_inc(hi_done, 1)

                square(0)
                square(1)
                for t in range(NT):
                    if t + 2 < NT:
                        square(t + 2)
                    high(t)

            @block.gpsimd
            def _(pool):
                def inverse_root(t):
                    pool.wait_ge(summed, t + 1)
                    nc.gpsimd.tensor_scalar(rs[:, t:t + 1], ss[:, t:t + 1], 1.0 / D, EPS, ALU.mult, ALU.add)
                    pool.drain()
                    nc.gpsimd.tensor_tensor(rs[:, t:t + 1], rs[:, t:t + 1], m["mhalf"][:, 0:1], ALU.pow).then_inc(root, 1)

                inverse_root(0)
                inverse_root(1)
                for t in range(NT):
                    if t + 2 < NT:
                        inverse_root(t + 2)
                    pool.wait_ge(hi_done, t + 1)
                    nc.gpsimd.tensor_tensor(h_lo[:, :, t * P:t * P + P], h[:, t % 2],
                                            h_hi[:, :, t * P:t * P + P].bitcast(F32), ALU.subtract).then_inc(lo_done, 1)

            @block.vector
            def _(dve):
                def scale(t):
                    dve.wait_ge(root, t + 1)
                    if t >= 2:
                        dve.wait_ge(turned, t - 1)
                    nc.vector.tensor_scalar(xn[:, t % 2, :], x[:, t % 3, :], rs[:, t:t + 1], None, ALU.mult).then_inc(scaled, 1)

                scale(0)
                for t in range(NT):
                    if t + 1 < NT:
                        scale(t + 1)
                    dve.wait_ge(turned, t + 1)
                    if t >= 2:
                        dve.wait_ge(lo_done, t - 1)
                    c = 1 if t == CTX else 0
                    for k in range(KD):
                        last = nc.vector.tensor_scalar(
                            h[:, t % 2, k, :], ps[:, 2 * (t % 2) + k // 4, P * (k % 4):P * (k % 4) + P],
                            m["scale"][:, k, c:c + 1], m["shift"][:, k, c:c + 1], ALU.mult, ALU.add)
                    last.then_inc(modulated, 1)

            @block.tensor
            def _(pe):
                for t in range(NT):
                    pe.wait_ge(scaled, t + 1)
                    if t >= 2:
                        pe.wait_ge(modulated, t - 1)
                    for k in range(KD):
                        last = nc.tensor.transpose(ps[:, 2 * (t % 2) + k // 4, P * (k % 4):P * (k % 4) + P],
                                                   xn[:, t % 2, P * k:P * k + P], m["ident"])
                    last.then_inc(turned, 1)
        clear(nc, sem)


def project_in(nc, io, m, l):
    with ExitStack() as ctx:
        sem = Sems(nc, ctx, "in")
        with nc.sbuf_tensor("in_w", [P, 3, KD, WC], F32) as wst:
            pass
        w_lo = ctx.enter_context(nc.sbuf_tensor("in_w_lo", [P, 3, KD, WC], F32R))
        w_hi = ctx.enter_context(nc.sbuf_tensor("in_w_hi", [P, 2, KD, WC], F32R))
        gate = ctx.enter_context(nc.sbuf_tensor("in_gate", [P, 3, GRP], F32))
        w_in = [sem(f"w_in{i}") for i in range(3)]
        g_out = [sem(f"g_out{i}") for i in range(3)]
        padded, lo_done, product, emptied = (
            sem("padded"), sem("lo_done"), sem("product"), sem("emptied"))
        ps, h_hi, h_lo, z, zc, zu = m["ps"], m["h_hi"], m["h_lo"], m["z"], m["zc"], m["zu"]
        w_dram = layer(io["w_in"], l).rearrange("(k p) n -> p k n", p=P)
        NB = 8

        def units(kind, cols):
            if kind == "tokens":
                return [(t, None) for t in range(NT)]
            return [(b, g) for b in range((cols + P - 1) // P) for g in range(T // GRP)]

        def products_before(i):
            return sum(len(units(kind, cols)) for _, cols, kind in CHUNKS[:i])

        with nc.Block() as block:
            @block.sync
            def _(sp):
                for i, (c0, cols, _) in enumerate(CHUNKS):
                    if i >= 3:
                        sp.wait_ge(product, products_before(i - 2))
                    sp.dma_start(wst[:, i % 3, :, 0:cols], w_dram[:, :, c0:c0 + cols]).then_inc(w_in[i % 3], 16)
                n = 0
                for i, (c0, cols, kind) in enumerate(CHUNKS):
                    if kind == "gate":
                        for j, (b, g) in enumerate(units(kind, cols)):
                            sp.wait_ge(emptied, products_before(i) + j + 1)
                            sp.dma_start(io["gates"][GATE_BLOCK[c0] + b, :, GRP * g:GRP * g + GRP],
                                         gate[:, n % 3, :]).then_inc(g_out[n % 3], 16)
                            n += 1
                for i in range(3):
                    sp.wait_ge(g_out[i], 16 * (n // 3))

            @block.gpsimd
            def _(pool):
                nc.gpsimd.memset(zc[:, :, 0:CPAD], 0.0)
                nc.gpsimd.memset(zc[:, :, CPAD + N_LAT:CPAD + N_LAT + 2], 0.0)
                nc.gpsimd.memset(zc[:, :, CW - 1:CW], 0.0)
                nc.gpsimd.memset(zu[:, :, 0:UPAD], 0.0)
                nc.gpsimd.memset(zu[:, :, UPAD + N_LAT:2 * UPAD + N_LAT], 0.0)
                nc.gpsimd.memset(zu[:, :, UW - UPAD:UW], 0.0).then_inc(padded, 1)

            @block.vector
            def _(dve):
                for i, (c0, cols, _) in enumerate(CHUNKS):
                    dve.wait_ge(w_in[i % 3], 16 * (i // 3 + 1))
                    if i >= 2:
                        dve.wait_ge(product, products_before(i - 1))
                    nc.vector.tensor_copy(w_hi[:, i % 2, :, 0:cols], wst[:, i % 3, :, 0:cols])
                    dve.drain()
                    nc.vector.tensor_tensor(w_lo[:, i % 3, :, 0:cols], wst[:, i % 3, :, 0:cols],
                                            w_hi[:, i % 2, :, 0:cols].bitcast(F32), ALU.subtract).then_inc(lo_done, 1)

            @block.tensor
            def _(pe):
                n = 0
                for i, (c0, cols, kind) in enumerate(CHUNKS):
                    pe.wait_ge(lo_done, i + 1)
                    w, v = i % 2, i % 3
                    for a, g in units(kind, cols):
                        if n >= NB:
                            pe.wait_ge(emptied, n - NB + 1)
                        if kind == "tokens":
                            rows = slice(P * a, P * a + P)
                            last = split3(nc, ps[:, n % NB, 0:cols],
                                          lambda k: h_hi[:, k, rows], lambda k: h_lo[:, k, rows],
                                          lambda k: w_hi[:, w, k, 0:cols], lambda k: w_lo[:, v, k, 0:cols], KD)
                        else:
                            mc = min(P, cols)
                            ch, tk = slice(P * a, P * a + mc), slice(GRP * g, GRP * g + GRP)
                            last = split3(nc, ps[0:mc, n % NB, 0:GRP],
                                          lambda k: w_hi[:, w, k, ch], lambda k: w_lo[:, v, k, ch],
                                          lambda k: h_hi[:, k, tk], lambda k: h_lo[:, k, tk], KD)
                        last.then_inc(product, 1)
                        n += 1

            @block.scalar
            def _(act):
                n = gates = 0
                act.wait_ge(padded, 1)
                for c0, cols, kind in CHUNKS:
                    for a, g in units(kind, cols):
                        act.wait_ge(product, n + 1)
                        src = ps[:, n % NB, :]
                        if kind == "tokens":
                            nc.scalar.activation(z[:, a, c0 - O_Q:c0 - O_Q + cols], src[:, 0:cols], ACT.Copy).then_inc(emptied, 1)
                        elif kind == "ba":
                            nc.scalar.activation(m["ba"][:, GRP * g:GRP * g + GRP], src[0:16, 0:GRP], ACT.Copy).then_inc(emptied, 1)
                        elif kind == "gate":
                            if gates >= 3:
                                act.wait_ge(g_out[gates % 3], 16 * (gates // 3))
                            nc.scalar.activation(gate[:, gates % 3, :], src[:, 0:GRP], ACT.Silu).then_inc(emptied, 1)
                            gates += 1
                        else:
                            dst, pad = (zc, CPAD) if kind == "delta" else (zu, UPAD)
                            b = (c0 - (O_DELTA if kind == "delta" else O_UPOOL)) // P + a
                            lat = min(GRP, N_LAT - GRP * g)
                            col = pad + GRP * g
                            last = nc.scalar.activation(dst[:, b, col:col + lat], src[:, 0:lat], ACT.Copy)
                            if lat < GRP:
                                last = nc.scalar.activation(dst[:, b, 2 * pad + N_LAT:2 * pad + T], src[:, lat:GRP], ACT.Copy)
                            last.then_inc(emptied, 1)
                        n += 1
        clear(nc, sem)


def prepare_tokens(nc, io, m, l):
    with ExitStack() as ctx:
        sem = Sems(nc, ctx, "tok")

        def sb(name, shape, dt=F32):
            return ctx.enter_context(nc.sbuf_tensor(f"tok_{name}", shape, dt))

        cv = sb("cv", [P, 6, CV])
        s2, s4 = sb("s2", [P, 2, UW]), sb("s4", [P, 2, UW])
        s8, s16 = sb("s8", [P, UW]), sb("s16", [P, UW])
        dpool = m["of"][:].rearrange("p t c -> p (t c)").rearrange("p (b t) -> p b t", t=T)
        inv = m["pbr"]
        rope = sb("rope", [P, 2, 8, HD])
        tab = sb("tab", [P, 4, HD])
        ra = sb("ra", [P, 10, HD])
        rb = sb("rb", [P, 10, HD])
        sqa, sqd = sb("sqa", [P, 640]), sb("sqd", [P, 512])
        ssa, ssd = sb("ssa", [P, NT, 10]), sb("ssd", [P, NT, 8])
        small = sb("small", [P, 8, NT, 8])
        tab_in = sem("tab_in")
        conv_done, silu_done, turned, tok_copied, sq_d, ss_d, root_d, unit_q, sq_a, ss_a, root_a = (
            sem("conv_done"), sem("silu_done"), sem("turned"), sem("tok_copied"), sem("sq_d"), sem("ss_d"),
            sem("root_d"), sem("unit_q"), sem("sq_a"), sem("ss_a"), sem("root_a"))
        ba_turned, ba_dve, ba_act, decay_mm, decay_dve, decay_act = (
            sem("ba_turned"), sem("ba_dve"), sem("ba_act"), sem("decay_mm"), sem("decay_dve"), sem("decay_act"))
        windows, pool_d, pool_mm, pool_out, finished = (
            sem("windows"), sem("pool_d"), sem("pool_mm"), sem("pool_out"), sem("finished"))
        ps, z, zc, zu, tok = m["ps"], m["z"], m["zc"], m["zu"], m["tok"]

        with nc.Block() as block:
            @block.sync
            def _(sp):
                sp.dma_start(inv[:], io["inv_count"]).then_inc(tab_in, 16)
                sp.dma_start(rope[:], io["rope"]).then_inc(tab_in, 16)
                sp.wait_ge(tab_in, 32)

            @block.tensor
            def _(pe):
                for t in range(NT):
                    last = nc.tensor.transpose(ps[:, 6, 16 * t:16 * t + 16], m["ba"][:, t * P:t * P + P],
                                               m["ident"][0:16, 0:16])
                last.then_inc(ba_turned, 1)
                pe.wait_ge(decay_dve, 1)
                g = m["g"]
                for d in range(2):
                    nc.tensor.matmul(ps[:, 7, 36 * d:36 * d + 36].rearrange("p (t h) -> p t h", h=4),
                                     m["masks"][:, M_INCL + d, :], g[:, :, 4 * d:4 * d + 4], start=True, stop=True)
                for c in range(2):
                    last = nc.tensor.matmul(ps[:, 7, 72 + 72 * c:144 + 72 * c].rearrange("p (t h) -> p t h", h=8),
                                            m["masks"][:, M_HALF + c, :], g[:], start=True, stop=True)
                last.then_inc(decay_mm, 1)
                for b in range(2):
                    pe.wait_ge(pool_d, b + 1)
                    for i in range(T // GRP):
                        n = 3 * b + i
                        if n >= 2:
                            pe.wait_ge(pool_out, n - 1)
                        nc.tensor.matmul(ps[:, 4 + n % 2, 0:GRP], m["poolw"][:, b, :], dpool[:, b, GRP * i:GRP * i + GRP],
                                         start=True, stop=True).then_inc(pool_mm, 1)
                pe.wait_ge(silu_done, 6)
                for t in range(NT):
                    if t >= 2:
                        pe.wait_ge(tok_copied, t - 1)
                    for b in range(6):
                        last = nc.tensor.transpose(ps[:, 2 * (t % 2) + b // 4, P * (b % 4):P * (b % 4) + P],
                                                   cv[:, b, cv_col(t):cv_col(t) + P], m["ident"])
                    last.then_inc(turned, 1)

            @block.scalar
            def _(act):
                act.wait_ge(ba_dve, 1)
                nc.scalar.activation(small[:, 3], small[:, 0], ACT.Exp, scale=-1.0)
                nc.scalar.activation(small[:, 4], small[:, 1], ACT.Exp)
                nc.scalar.activation(m["ea"][:], m["alog"], ACT.Exp)
                act.drain()
                nc.scalar.activation(small[:, 5], small[:, 4], ACT.Ln, bias=1.0).then_inc(ba_act, 1)
                act.wait_ge(decay_dve, 2)
                act.wait_ge(decay_mm, 1)
                for d in range(2):
                    nc.scalar.activation(m["eg"][:, :, 4 * d:4 * d + 4],
                                         ps[:, 7, 36 * d:36 * d + 36].rearrange("p (t h) -> p t h", h=4), ACT.Exp)
                nc.scalar.activation(m["ekd"][:], small[:, 6], ACT.Exp)
                for c in range(2):
                    for half in range(2):
                        src = ps[64 * half:64 * half + 64, 7, 72 + 72 * c:144 + 72 * c]
                        last = nc.scalar.activation(
                            m["egl"][64 * half:64 * half + 64, c].rearrange("p t d h -> p (t d h)"),
                            src.rearrange("p (x two) -> p x two", two=2)[:, :, half], ACT.Exp)
                last.then_inc(decay_act, 1)
                for b in range(2):
                    for i in range(T // GRP):
                        act.wait_ge(pool_mm, 3 * b + i + 1)
                        nc.scalar.activation(m["pbr"][:, b, GRP * i:GRP * i + GRP], ps[:, 4 + (3 * b + i) % 2, 0:GRP],
                                             ACT.Copy, scale=m["psc"][:, b:b + 1]).then_inc(pool_out, 1)
                for b in range(6):
                    act.wait_ge(conv_done, b + 1)
                    nc.scalar.activation(cv[:, b, :], cv[:, b, :], ACT.Silu).then_inc(silu_done, 1)
                for t in range(NT):
                    act.wait_ge(turned, t + 1)
                    nc.scalar.activation(tok[:, t, 0:512], ps[:, 2 * (t % 2), :], ACT.Copy)
                    nc.scalar.activation(tok[:, t, 512:768], ps[:, 2 * (t % 2) + 1, 0:256], ACT.Copy).then_inc(tok_copied, 1)

            @block.gpsimd
            def _(pool):
                for t in range(NT):
                    if t >= 1:
                        pool.wait_ge(ss_a, t)
                    nc.gpsimd.tensor_tensor(sqa[:], z[:, t, 0:640], z[:, t, 0:640], ALU.mult).then_inc(sq_a, 1)
                pool.wait_ge(ss_a, NT)
                nc.gpsimd.tensor_scalar(ssa[:], ssa[:], 1.0 / HD, EPS, ALU.mult, ALU.add)
                pool.drain()
                nc.gpsimd.tensor_tensor(ssa[:], ssa[:], m["mhalf"][:, 0:90].rearrange("p (t h) -> p t h", h=10),
                                        ALU.pow).then_inc(root_a, 1)
                nc.gpsimd.tensor_tensor(s2[:, :, 0:UW - 1], zu[:, :, 0:UW - 1], zu[:, :, 1:UW], ALU.add)
                pool.drain()
                nc.gpsimd.tensor_tensor(s4[:, :, 0:UW - 3], s2[:, :, 0:UW - 3], s2[:, :, 2:UW - 1], ALU.add)
                pool.drain()
                nc.gpsimd.tensor_tensor(s8[:, 0:UW - 7], s4[:, 1, 0:UW - 7], s4[:, 1, 4:UW - 3], ALU.add)
                pool.drain()
                nc.gpsimd.tensor_tensor(s16[:, 0:UW - 15], s8[:, 0:UW - 15], s8[:, 8:UW - 7], ALU.add)
                pool.drain()
                pool.wait_ge(tab_in, 32)
                sums = (s2[0:64, 0], s4[64:128, 0], s8[0:64], s16[64:128])
                for g in range(4):
                    b, h = g // 2, slice(64 * (g % 2), 64 * (g % 2) + 64)
                    for s, (t0, n) in enumerate(SEQS):
                        u0 = UPAD * (s + 1) + t0
                        a = u0 - WINDOWS[g] // 2
                        nc.gpsimd.tensor_tensor(dpool[h, b, t0:t0 + n], sums[g][:, a:a + n], inv[h, b, t0:t0 + n], ALU.mult)
                pool.drain()
                for b in range(2):
                    for s, (t0, n) in enumerate(SEQS):
                        u0 = UPAD * (s + 1) + t0
                        last = nc.gpsimd.tensor_tensor(dpool[:, b, t0:t0 + n], dpool[:, b, t0:t0 + n],
                                                       zu[:, b, u0:u0 + n], ALU.subtract)
                    last.then_inc(pool_d, 1)
                for t in range(NT):
                    pool.wait_ge(tok_copied, t + 1)
                    if t >= 1:
                        pool.wait_ge(ss_d, t)
                    nc.gpsimd.tensor_tensor(sqd[:], tok[:, t, 0:512], tok[:, t, 0:512], ALU.mult).then_inc(sq_d, 1)
                pool.wait_ge(ss_d, NT)
                nc.gpsimd.tensor_scalar(ssd[:], ssd[:], 1.0, EPS, ALU.mult, ALU.add)
                pool.drain()
                nc.gpsimd.tensor_tensor(ssd[:], ssd[:], m["mhalf"][:, 0:72].rearrange("p (t h) -> p t h", h=8),
                                        ALU.pow)
                pool.drain()
                nc.gpsimd.tensor_scalar(ssd[:, :, 0:4], ssd[:, :, 0:4], HD ** -0.5, None, ALU.mult)
                pool.drain()
                for t in range(NT):
                    qk = tok[:, t, 0:512].rearrange("p (h d) -> p h d", d=HD)
                    nc.gpsimd.tensor_tensor(qk, qk, ssd[:, t, :].unsqueeze(2).broadcast_to([P, 8, HD]), ALU.mult)
                pool.drain()

            @block.vector
            def _(dve):
                dve.wait_ge(ba_turned, 1)
                ba = ps[:, 6, 0:144].rearrange("p (t c) -> p t c", c=16)
                nc.vector.tensor_copy(small[:, 0], ba[:, :, 0:8])
                nc.vector.tensor_tensor(small[:, 2], ba[:, :, 8:16],
                                        m["dtb"].unsqueeze(1).broadcast_to([P, NT, 8]), ALU.add)
                dve.drain()
                nc.vector.tensor_scalar(small[:, 1], small[:, 2], -1.0, None, ALU.mult)
                dve.drain()
                nc.vector.tensor_tensor(small[:, 1], small[:, 1], small[:, 2], ALU.min).then_inc(ba_dve, 1)
                dve.wait_ge(ba_act, 1)
                nc.vector.tensor_scalar(small[:, 3], small[:, 3], 1.0, None, ALU.add)
                nc.vector.scalar_tensor_tensor(out=small[:, 5], in0=small[:, 2], scalar=0.0, in1=small[:, 5],
                                               op0=ALU.max, op1=ALU.add)
                dve.drain()
                nc.vector.reciprocal(m["beta"][:], small[:, 3])
                nc.vector.scalar_tensor_tensor(out=m["g"][:], in0=small[:, 5], scalar=-1.0,
                                               in1=m["ea"][:].unsqueeze(1).broadcast_to([P, NT, 8]),
                                               op0=ALU.mult, op1=ALU.mult).then_inc(decay_dve, 1)
                dve.wait_ge(decay_mm, 1)
                for d in range(2):
                    nc.vector.tensor_copy(m["gc"][:, :, 4 * d:4 * d + 4],
                                          ps[:, 7, 36 * d:36 * d + 36].rearrange("p (t h) -> p t h", h=4))
                dve.drain()
                for c in range(2):
                    h = slice(64 * c, 64 * c + 64)
                    last = nc.vector.tensor_tensor(small[h, 6], ps[h, 7, 72 + 72 * c:144 + 72 * c]
                                                   .rearrange("p (t h) -> p t h", h=8), m["gc"][h], ALU.subtract)
                last.then_inc(decay_dve, 1)
                for t in range(NT):
                    dve.wait_ge(sq_a, t + 1)
                    nc.vector.tensor_reduce(ssa[:, t, :], sqa[:].rearrange("p (h d) -> p h d", d=HD), AX_X,
                                            ALU.add).then_inc(ss_a, 1)
                for b in range(6):
                    nc.vector.tensor_scalar(cv[:, b, :], zc[:, b, 0:CV], m["convw"][:, 0, b:b + 1], None, ALU.mult)
                for j in range(1, 4):
                    dve.drain()
                    for b in range(6):
                        last = nc.vector.scalar_tensor_tensor(out=cv[:, b, :], in0=zc[:, b, j:j + CV],
                                                              scalar=m["convw"][:, j, b:b + 1], in1=cv[:, b, :],
                                                              op0=ALU.mult, op1=ALU.add)
                        if j == 3:
                            last.then_inc(conv_done, 1)
                dve.wait_ge(decay_act, 1)
                nc.vector.tensor_tensor(m["beg"][:], m["beta"][:], m["eg"][:], ALU.mult)
                dve.wait_ge(root_a, 1)
                dve.wait_ge(tab_in, 32)

                def rotary(t):
                    q = z[:, t, 0:640].rearrange("p (h d) -> p h d", d=HD)
                    if t != CTX:
                        for i, w in enumerate((m["qn"], m["kn"])):
                            nc.vector.tensor_tensor(tab[:, i], rope[:, 0, t], w, ALU.mult)
                            pairs = w.rearrange("p (d two) -> p d two", two=2)[:, :, ::-1]
                            nc.vector.tensor_tensor(tab[:, 2 + i].rearrange("p (d two) -> p d two", two=2),
                                                    rope[:, 1, t].rearrange("p (d two) -> p d two", two=2), pairs, ALU.mult)
                    nc.vector.tensor_tensor(ra[:], q, ssa[:, t, :].unsqueeze(2).broadcast_to([P, 10, HD]), ALU.mult)
                    dve.drain()
                    parts = ((0, 8, 0), (8, 10, 1))
                    if t == CTX:
                        for (h0, h1, i), w in zip(parts, (m["qn"], m["kn"])):
                            nc.vector.tensor_tensor(q[:, h0:h1], ra[:, h0:h1],
                                                    w.unsqueeze(1).broadcast_to([P, h1 - h0, HD]), ALU.mult)
                        return
                    for h0, h1, i in parts:
                        nc.vector.tensor_tensor(q[:, h0:h1], ra[:, h0:h1],
                                                tab[:, i].unsqueeze(1).broadcast_to([P, h1 - h0, HD]), ALU.mult)
                        for e in range(2):
                            nc.vector.tensor_tensor(
                                rb[:, h0:h1].rearrange("p h (d two) -> p h d two", two=2)[:, :, :, e],
                                ra[:, h0:h1].rearrange("p h (d two) -> p h d two", two=2)[:, :, :, 1 - e],
                                tab[:, 2 + i].rearrange("p (d two) -> p d two", two=2)[:, :, e].unsqueeze(1)
                                .broadcast_to([P, h1 - h0, HD // 2]), ALU.mult)
                    dve.drain()
                    nc.vector.tensor_tensor(q, q, rb[:], ALU.add)

                for t in range(NT):
                    rotary(t)
                for t in range(NT):
                    dve.wait_ge(sq_d, t + 1)
                    nc.vector.tensor_reduce(ssd[:, t, :], sqd[:].rearrange("p (h d) -> p h d", d=HD), AX_X,
                                            ALU.add).then_inc(ss_d, 1)
        clear(nc, sem)


HEAD = ["k", "q", "gc", "ev", "od", "t0"]
STEPS = NT
TURN = [(0, "x1"), (0, "y1"), ("a", 0), (0, "r1"), (1, "k"), (1, "q"), ("b", 0), (0, "x2"), (0, "y2"), ("c", 0),
        (0, "r2"), (1, "gc"), ("a", 1), (0, "x3"), (0, "y3"), ("b", 1), (0, "r3"), ("c", 1), (1, "ev"), (1, "od"),
        (0, "x4"), (0, "y4"), (0, "r4"), (0, "x5"), (0, "z5"), (1, "t0")]


def delta_order(phase, scan):
    for name in HEAD:
        phase(0, name)
    for j in range(STEPS + 1):
        for what, which in TURN:
            if what in (0, 1):
                if j + what < STEPS:
                    phase(j + what, which)
            elif j >= 1:
                scan(j - 1, what, which)


def batch_numbers():
    order = []
    delta_order(lambda j, name: order.extend((j, name, d) for d in range(2)), lambda *a: None)
    return {what: n for n, what in enumerate(order)}


BATCH = batch_numbers()


def delta_tile(j, d):
    return CTX if j == 0 else (j - 1 if d == 0 else NT - 1 - j)


def batch(j, phase, d):
    return BATCH[j, phase, d]


def state_in(s):
    return s if s < 3 else 1 if s % 2 else 2


def state_out(s):
    return 0 if s == 1 else state_in(s + 1)


def delta_rule(nc, io, m, l):
    with ExitStack() as ctx:
        sem = Sems(nc, ctx, "delta")

        def sb(name, shape):
            return [ctx.enter_context(nc.sbuf_tensor(f"delta_{name}{d}", shape, F32)) for d in range(2)]

        kb, qg = sb("kb", [P, 4, HD]), sb("qg", [P, 4, HD])
        kd, bv = sb("kd", [P, 3, 4, HD]), sb("bv", [P, 3, 4, HD])
        KT, QT = sb("KT", [P, 3, 4, P]), sb("QT", [P, 3, 4, P])
        zc = m["zc"].rearrange("p b c -> p (b c)")
        E = [zc[:, 1024 * d:1024 * d + 1024].rearrange("p (n h c) -> p n h c", n=2, c=P) for d in range(2)]
        AT = [zc[:, 2048 + 1536 * d:3584 + 1536 * d].rearrange("p (n h c) -> p n h c", n=3, c=P) for d in range(2)]
        ML = sb("ML", [P, 2, 4, P])
        Ti, X, R = sb("T", [P, 4, P]), sb("X", [P, 4, P]), sb("R", [P, 2, 4, P])
        kS, rr, vn = sb("kS", [P, 4, HD]), sb("rr", [P, 4, HD]), sb("vn", [P, 4, HD])
        S, Sg = sb("S", [P, 3, 2, HD]), sb("Sg", [P, 2, HD])
        s_in = sem("s_in")
        zeroed, scaled, product = sem("zeroed"), sem("scaled"), sem("product")
        emptied = [sem(f"emptied{i}") for i in range(4)]
        e_done, masked, r0_done, ml_done = sem("e_done"), sem("masked"), sem("r0_done"), sem("ml_done")
        a_mm, r_done, b_mm, vn_done, s_mm, o_mm, s_done, o_done = (
            [sem(f"{n}{d}") for d in range(2)] for n in ("a_mm", "r_done", "b_mm", "vn_done", "s_mm", "o_mm", "s_done", "o_done"))
        state_out_done = sem("state_out")
        ps, tok, masks = m["ps"], m["tok"], m["masks"]
        o = [m["of"], m["ob"]]

        def bank(j, phase, d):
            return ps[:, batch(j, phase, d) % 4, :].rearrange("p (h c) -> p h c", c=P)

        def is_emptied(eng, j, phase, d):
            n = batch(j, phase, d)
            eng.wait_ge(emptied[n % 4], n // 4 + 1)

        def is_product(eng, j, phase, d):
            eng.wait_ge(product, batch(j, phase, d) + 1)

        def empty_inc(ins, j, phase, d):
            ins.then_inc(emptied[batch(j, phase, d) % 4], 1)

        def heads(t, base, h):
            return tok[:, t, base + HD * h:base + HD * h + HD]

        def rows(c):
            return slice(64 * c, 64 * c + 64)

        def chunk(c2, d):
            return c2 if d == 0 else 1 - c2

        def level_mask(i, d):
            return masks[:, M_LEVEL + LEVELS * d + i, :]

        with nc.Block() as block:
            @block.sync
            def _(sp):
                for d in range(2):
                    sp.dma_start(S[d][:, 2], layer(io["state_delta"], l)[4 * HD * d:4 * HD * d + 4 * HD, :]
                                 .rearrange("(pair x) v -> x pair v", x=P)).then_inc(s_in, 16)
                for d in range(2):
                    sp.wait_ge(s_done[d], 2)
                    sp.dma_start(layer(io["new_state"], l)[4 * HD * d:4 * HD * d + 4 * HD, :]
                                 .rearrange("(pair x) v -> x pair v", x=P), S[d][:, 0]).then_inc(state_out_done, 16)
                sp.wait_ge(state_out_done, 32)

            @block.gpsimd
            def _(pool):
                for d in range(2):
                    last = nc.gpsimd.memset(S[d][:, 0], 0.0)
                last.then_inc(zeroed, 1)

                def scale_tokens(j, d):
                    t, jj = delta_tile(j, d), j % 3
                    if j >= 1:
                        is_product(pool, j - 1, "q", d)
                    if j >= 3:
                        pool.wait_ge(o_mm[d], 2 * (j - 2))

                    def by(x):
                        return x[:, t, 4 * d:4 * d + 4].unsqueeze(2).broadcast_to([P, 4, HD])

                    q, k, v = (tok[:, t, 256 * i:256 * i + 256].rearrange("p (h e) -> p h e", e=HD) for i in range(3))
                    nc.gpsimd.tensor_tensor(kb[d][:], k, by(m["beta"]), ALU.mult)
                    nc.gpsimd.tensor_tensor(qg[d][:], q, by(m["eg"]), ALU.mult)
                    nc.gpsimd.tensor_tensor(kd[d][:, jj], k, by(m["ekd"]), ALU.mult)
                    nc.gpsimd.tensor_tensor(bv[d][:, jj], v, by(m["beta"]), ALU.mult).then_inc(scaled, 1)

                def mask_level(j, i):
                    for d in range(2):
                        if i >= 3:
                            is_product(pool, j, f"x{i - 2}", d)
                        elif j >= 1:
                            is_product(pool, j - 1, "x5" if i == 1 else "x4", d)
                        nc.gpsimd.tensor_tensor(ML[d][:, i % 2], E[d][:, j % 2], level_mask(i, d).unsqueeze(1)
                                                .broadcast_to([P, 4, P]), ALU.mult).then_inc(ml_done, 1)

                def phase(j, name):
                    if name == "gc":
                        for d in range(2):
                            pool.wait_ge(e_done, 2 * j + d + 1)
                            if j >= 3:
                                pool.wait_ge(o_mm[d], 2 * (j - 2))
                            nc.gpsimd.tensor_tensor(AT[d][:, j % 3], E[d][:, j % 2], masks[:, M_INCL + d, :].unsqueeze(1)
                                                    .broadcast_to([P, 4, P]), ALU.mult)
                            pool.drain()
                            nc.gpsimd.tensor_tensor(E[d][:, j % 2], E[d][:, j % 2], masks[:, M_STRICT + d, :].unsqueeze(1)
                                                    .broadcast_to([P, 4, P]), ALU.mult).then_inc(masked, 1)
                    elif name == "od":
                        for d in range(2):
                            is_emptied(pool, j, "ev", d)
                            is_emptied(pool, j, "od", d)
                            if j >= 2:
                                pool.wait_ge(b_mm[d], 2 * (j - 1))
                            r0 = R[d][:, j % 2]
                            nc.gpsimd.tensor_tensor(r0, E[d][:, j % 2], level_mask(0, d).unsqueeze(1).broadcast_to([P, 4, P]), ALU.mult)
                            pool.drain()
                            nc.gpsimd.tensor_tensor(r0, m["ident"].unsqueeze(1).broadcast_to([P, 4, P]), r0,
                                                    ALU.subtract).then_inc(r0_done, 1)
                    elif name == "t0":
                        mask_level(j, 1)
                        mask_level(j, 2)
                        if j + 1 < STEPS:
                            for d in range(2):
                                scale_tokens(j + 1, d)
                    elif name in ("x1", "x2", "x3"):
                        mask_level(j, int(name[1]) + 2)

                for d in range(2):
                    scale_tokens(0, d)
                delta_order(phase, lambda *a: None)

            @block.tensor
            def _(pe):
                def transposes(j, phase, d, sources, w=P):
                    for i, src in enumerate(sources):
                        last = nc.tensor.transpose(bank(j, phase, d)[:, i, :], src, m["ident"])
                    last.then_inc(product, 1)

                def products(j, phase, d, lhs, rhs):
                    for h in range(NDH):
                        last = nc.tensor.matmul(bank(j, phase, d)[:, h, :], lhs(h), rhs(h), start=True, stop=True)
                    last.then_inc(product, 1)

                def phase_products(j, phase, d):
                    n = batch(j, phase, d)
                    t, jj, j3 = delta_tile(j, d), j % 2, j % 3
                    if n >= 4:
                        pe.wait_ge(emptied[n % 4], n // 4)
                    kind, i = phase[0], int(phase[1]) if phase[1:].isdigit() else 0
                    if phase == "k":
                        pe.wait_ge(scaled, 2 * j + d + 1)
                        transposes(j, phase, d, [tok[:, t, 256 + P * p:256 + P * p + P] for p in range(2)]
                                   + [kb[d][:].rearrange("p h e -> p (h e)")[:, P * p:P * p + P] for p in range(2)])
                    elif phase == "q":
                        transposes(j, phase, d, [tok[:, t, P * p:P * p + P] for p in range(2)]
                                   + [qg[d][:].rearrange("p h e -> p (h e)")[:, P * p:P * p + P] for p in range(2)])
                    elif phase == "gc":
                        products(j, phase, d, lambda h: m["g"][:, t, 4 * d + h:4 * d + h + 1].broadcast_to([P, P]),
                                 lambda h: masks[:, M_INCL + d, :])
                    elif phase in ("ev", "od"):
                        is_emptied(pe, j, "k", d)
                        is_emptied(pe, j, "q", d)
                        p = 64 * (phase == "od")
                        for x in range(2):
                            for i2 in range(2):
                                rhs = (KT[d], 2) if x == 0 else (QT[d], 0)
                                last = nc.tensor.matmul(bank(j, phase, d)[:, 2 * x + i2, :], KT[d][p:p + 64, j3, i2, :],
                                                        rhs[0][p:p + 64, j3, rhs[1] + i2, :], start=True, stop=True)
                        last.then_inc(product, 1)
                    elif phase == "t0":
                        pe.wait_ge(r0_done, 2 * j + d + 1)
                        transposes(j, phase, d, [R[d][:, jj, h, :] for h in range(NDH)])
                    elif kind == "x":
                        is_emptied(pe, j, "t0" if i == 1 else f"y{i - 1}", d)
                        pe.wait_ge(ml_done, (LEVELS - 1) * 2 * j + 2 * (i - 1) + d + 1)
                        products(j, phase, d, lambda h: ML[d][:, i % 2, h, :], lambda h: Ti[d][:, h, :])
                    elif kind == "y":
                        is_emptied(pe, j, f"x{i}", d)
                        if i > 1:
                            is_emptied(pe, j, f"r{i - 1}", d)
                        products(j, phase, d, lambda h: R[d][:, jj, h, :], lambda h: X[d][:, h, :])
                    elif kind == "r":
                        is_emptied(pe, j, f"y{i}", d)
                        transposes(j, phase, d, [Ti[d][:, h, :] for h in range(NDH)])
                    else:
                        is_emptied(pe, j, "x5", d)
                        is_emptied(pe, j, "r4", d)
                        products(j, phase, d, lambda h: X[d][:, h, :], lambda h: R[d][:, jj, h, :])

                def scan(j, part, c2):
                    s, jj, j3 = 2 * j + c2, j % 2, j % 3
                    for d in range(2):
                        r = rows(chunk(c2, d))
                        state = lambda h: S[d][64 * (h % 2):64 * (h % 2) + 64, state_in(s), h // 2, :]
                        half = lambda x, i: (lambda h: x[64 * (h % 2):64 * (h % 2) + 64, j3, i + h // 2, r])
                        bank_a = ps[:, 4 + 2 * d, :].rearrange("p (h e) -> p h e", e=HD)
                        bank_b = ps[:, 5 + 2 * d, :].rearrange("p (h e) -> p h e", e=HD)
                        if part == "a":
                            if s == 0:
                                pe.wait_ge(zeroed, 1)
                            elif s == 2:
                                pe.wait_ge(s_in, 32)
                            if s > 0:
                                pe.wait_ge(s_done[d], s)
                            for h in (0, 2, 1, 3):
                                if h == 1:
                                    pe.drain()
                                last = nc.tensor.matmul(bank_a[r, h, :], half(KT[d], 0)(h), state(h), start=True, stop=True)
                            last.then_inc(a_mm[d], 1)
                        elif part == "b":
                            pe.wait_ge(r_done[d], s + 1)
                            if s > 0:
                                pe.wait_ge(o_done[d], s)
                            if c2 == 0:
                                is_emptied(pe, j, "z5", d)
                            for h in range(NDH):
                                last = nc.tensor.matmul(bank_b[r, h, :], R[d][r, jj, h, r], rr[d][r, h, :], start=True, stop=True)
                            last.then_inc(b_mm[d], 1)
                        else:
                            pe.wait_ge(vn_done[d], s + 1)
                            for h in range(NDH):
                                q = slice(64 * (h % 2), 64 * (h % 2) + 64)
                                last = nc.tensor.matmul(bank_a[q, 4 + h // 2, :], kd[d][r, j3, h, :], vn[d][r, h, :],
                                                        start=True, stop=True)
                            last.then_inc(s_mm[d], 1)
                            for h in (0, 2, 1, 3):
                                if h == 1:
                                    pe.drain()
                                nc.tensor.matmul(bank_b[r, 4 + h, :], half(QT[d], 2)(h), state(h), start=(h == 0), stop=False,
                                                 skip_group_check=True)
                            pe.drain()
                            for h in range(NDH):
                                last = nc.tensor.matmul(bank_b[r, 4 + h, :], AT[d][r, j3, h, r], vn[d][r, h, :],
                                                        start=False, stop=(h == NDH - 1), skip_group_check=True)
                            last.then_inc(o_mm[d], 1)

                delta_order(lambda j, name: [phase_products(j, name, d) for d in range(2)], scan)

            @block.scalar
            def _(act):
                def empty(j, phase, d):
                    jj = j % 2
                    if phase in ("k", "q") and j >= 3:
                        act.wait_ge(o_mm[d], 2 * (j - 2))
                    dst = {"k": KT[d][:, j % 3], "q": QT[d][:, j % 3], "t": Ti[d][:], "x": X[d][:], "r": R[d][:, jj]}[phase[0]]
                    is_product(act, j, phase, d)
                    empty_inc(nc.scalar.activation(dst, bank(j, phase, d), ACT.Copy), j, phase, d)

                def scan(j, part, c2):
                    s = 2 * j + c2
                    for d in range(2):
                        t, r = delta_tile(j, d), rows(chunk(c2, d))
                        bank_b = ps[:, 5 + 2 * d, :].rearrange("p (h e) -> p h e", e=HD)
                        if part == "b":
                            act.wait_ge(b_mm[d], s + 1)
                            nc.scalar.activation(vn[d][r], bank_b[r, 0:4, :], ACT.Copy).then_inc(vn_done[d], 1)
                        elif part == "c":
                            act.wait_ge(o_mm[d], s + 1)
                            nc.scalar.activation(o[d][r, t, :].rearrange("p (h e) -> p h e", e=HD), bank_b[r, 4:8, :],
                                                 ACT.Copy).then_inc(o_done[d], 1)

                def phase(j, name):
                    for d in range(2):
                        if name[0] in "kqtxr":
                            empty(j, name, d)
                        elif name == "gc":
                            is_emptied(act, j, "gc", d)
                            nc.scalar.activation(E[d][:, j % 2], E[d][:, j % 2], ACT.Exp).then_inc(e_done, 1)

                delta_order(phase, scan)

            @block.vector
            def _(dve):
                def empty(j, phase, d):
                    t, jj = delta_tile(j, d), j % 2
                    if phase == "gc":
                        is_product(dve, j, phase, d)
                        if j >= 2:
                            dve.wait_ge(ml_done, (LEVELS - 1) * 2 * (j - 1))
                        for h in range(NDH):
                            last = nc.vector.tensor_scalar(E[d][:, j % 2, h, :], bank(j, phase, d)[:, h, :],
                                                           m["gc"][:, t, 4 * d + h:4 * d + h + 1], 0.0,
                                                           ALU.subtract, ALU.min)
                    elif phase in ("ev", "od"):
                        dve.wait_ge(masked, 2 * j + d + 1)
                        is_product(dve, j, phase, d)
                        p, b = int(phase == "od"), bank(j, phase, d)
                        nc.vector.tensor_tensor(E[d][:, jj, p::2], b[:, 0:2], E[d][:, jj, p::2], ALU.mult)
                        last = nc.vector.tensor_tensor(AT[d][:, j % 3, p::2], b[:, 2:4], AT[d][:, j % 3, p::2], ALU.mult)
                    elif phase[0] == "y":
                        is_product(dve, j, phase, d)
                        last = nc.vector.tensor_tensor(Ti[d][:], Ti[d][:], bank(j, phase, d), ALU.subtract)
                    else:
                        is_product(dve, j, phase, d)
                        last = nc.vector.tensor_tensor(R[d][:, jj], R[d][:, jj], bank(j, phase, d), ALU.subtract)
                    empty_inc(last, j, phase, d)

                def scan(j, part, c2):
                    s = 2 * j + c2
                    for d in range(2):
                        t, c = delta_tile(j, d), chunk(c2, d)
                        r = rows(c)
                        bank_a = ps[:, 4 + 2 * d, :].rearrange("p (h e) -> p h e", e=HD)
                        if part == "a":
                            dve.wait_ge(a_mm[d], s + 1)
                            nc.vector.tensor_tensor(kS[d][r], bank_a[r, 0:4, :],
                                                    m["beg"][r, t, 4 * d:4 * d + 4].unsqueeze(2).broadcast_to([64, 4, HD]),
                                                    ALU.mult)
                            nc.vector.tensor_tensor(Sg[d][:], S[d][:, state_in(s)],
                                                    m["egl"][:, c, t, d, :].unsqueeze(2).broadcast_to([P, 2, HD]), ALU.mult)
                            dve.drain()
                            nc.vector.tensor_tensor(rr[d][r], bv[d][r, j % 3], kS[d][r], ALU.subtract).then_inc(r_done[d], 1)
                        elif part == "c":
                            dve.wait_ge(s_mm[d], s + 1)
                            nc.vector.tensor_tensor(S[d][:, state_out(s)], Sg[d][:], bank_a[:, 4:6, :], ALU.add).then_inc(s_done[d], 1)

                def phase(j, name):
                    for d in range(2):
                        if name in ("gc", "ev", "od", "z5") or name[0] == "y":
                            empty(j, name, d)

                delta_order(phase, scan)
        clear(nc, sem)


LAT_KEYS = N_LAT + P
N_KEYS = LAT_KEYS + N_CTX
QB = 512
UNITS = ([(b * 4, 4, 0, LAT_KEYS // P, g) for b in range(N_LAT // QB) for g in range(NKV)]
         + [(CTX, 1, LAT_KEYS // P, 1, g) for g in range(NKV)])
ASKS = [(u, i) for u in range(len(UNITS)) for i in range(UNITS[u][1])]


def attention_order(hi, maxima, lo, first, step, last):
    def ready(u, i):
        hi(u, i)
        for h in range(Q_PER_KV):
            maxima(u, i, h)
        lo(u, i)

    for i in range(UNITS[0][1]):
        ready(0, i)
    for u, (_, _, _, keys, _) in enumerate(UNITS):
        nxt = u + 1 if u + 1 < len(UNITS) else None
        small = keys == 1
        if small and nxt is not None:
            ready(nxt, 0)
            nxt = None
        if small and u == len(UNITS) - 1:
            nxt = None
        for h in range(Q_PER_KV):
            first(u, h)
            for kt in range(keys):
                if nxt is not None:
                    if h < UNITS[nxt][1]:
                        if kt == 0:
                            hi(nxt, h)
                        elif kt <= Q_PER_KV:
                            maxima(nxt, h, kt - 1)
                    if kt == 6 and h < UNITS[nxt][1]:
                        lo(nxt, h)
                step(u, h, kt)
            last(u, h)


def turn_order():
    order = [("k", kt) for kt in range(N_KEYS // P)] + [("o", t) for t in range(NT)]
    none = lambda *a: None
    attention_order(lambda u, i: order.append(("hi", u, i)), none, lambda u, i: order.append(("lo", u, i)),
                    none, none, none)
    return {what: n for n, what in enumerate(order)}


def attention(nc, io, m, l):
    with ExitStack() as ctx:
        sem = Sems(nc, ctx, "attn")

        def sb(name, shape, dt=F32):
            return ctx.enter_context(nc.sbuf_tensor(f"attn_{name}", shape, dt))

        KH, KO = sb("KH", [P, NKV, N_KEYS], F32R), sb("KO", [P, NKV, N_KEYS], F32R)
        V = sb("V", [P, N_KEYS // P, NKV, P])
        ck, cvv = sb("ck", [P, NKV * HD]), sb("cv", [P, NKV * HD])
        khl = sb("khl", [P, 2, NKV, P])
        QH, QL = sb("QH", [P, 2, Q_PER_KV, QB], F32R), sb("QL", [P, 2, Q_PER_KV, QB], F32R)
        qhh, ql = sb("qhh", [P, 2, Q_PER_KV, P]), sb("ql", [P, 2, Q_PER_KV, HD + 2])
        m3, mx = sb("m3", [P, 2, Q_PER_KV, 3]), sb("mx", [P, 2, Q_PER_KV])
        pr = sb("pr", [P, 3, QB])
        rc = sb("rc", [P, 2, QB])
        osq, oss = sb("osq", [P, 2, 256]), sb("oss", [P, NT, 4])
        cache_in, kv_out = sem("cache_in"), sem("kv_out")
        ones_done, k_split, v_done = sem("ones_done"), sem("k_split"), sem("v_done")
        turned, turn_copied = sem("turned"), sem("turn_copied")
        o_sum, o_sq, o_ss, o_root, o_norm, o_ready = (sem(n) for n in ("o_sum", "o_sq", "o_ss", "o_root", "o_norm", "o_ready"))
        q_split, m_done, mx_product, mx_read = sem("q_split"), sem("m_done"), sem("mx_product"), sem("mx_read")
        st_done, p_done, pv_done, o_done = sem("st_done"), sem("p_done"), sem("pv_done"), sem("o_done")
        ps, z, br, of, ob = m["ps"], m["z"], m["zc"], m["of"], m["ob"]
        turn = turn_order()
        KTL = N_KEYS // P

        def keys_of(kt):
            return ck[:] if kt == KTL - 2 else z[:, CTX if kt == KTL - 1 else kt, 512:640]

        def is_turned(eng, *what):
            eng.wait_ge(turned, turn[what] + 1)

        def is_turn_copied(eng, *what):
            eng.wait_ge(turn_copied, turn[what] + 1)

        def chunks(u):
            _, _, k0, keys, _ = UNITS[u]
            w = min(keys * P, GRP)
            return [(k0 * P + a, w) for a in range(0, keys * P, w)]

        mx_before = {}
        n = 0
        def count(u, i, h):
            nonlocal n
            mx_before[u, i, h] = n
            n += len(chunks(u))
        none = lambda *a: None
        attention_order(none, count, none, none, none, none)
        st_before, n = {}, 0
        for u, (_, _, _, keys, _) in enumerate(UNITS):
            for h in range(Q_PER_KV):
                for kt in range(keys):
                    st_before[u, h, kt] = n
                    n += 1
        steps = list(st_before)

        with nc.Block() as block:
            @block.sync
            def _(sp):
                sp.dma_start(ck[:], layer(io["cache_k"], l)).then_inc(cache_in, 16)
                sp.dma_start(cvv[:], layer(io["cache_v"], l)).then_inc(cache_in, 16)
                sp.dma_start(layer(io["new_k"], l), z[:, CTX, 512:640]).then_inc(kv_out, 16)
                sp.dma_start(layer(io["new_v"], l), z[:, CTX, 640:768]).then_inc(kv_out, 16)
                sp.wait_ge(kv_out, 32)

            @block.gpsimd
            def _(pool):
                nc.gpsimd.memset(V[:, :, :, HD:P], 1.0)
                pool.drain()
                nc.gpsimd.memset(KO[HD:HD + 1].bitcast(F32), 1.0).then_inc(ones_done, 1)
                pool.drain()
                pool.wait_ge(cache_in, 32)
                for kt in range(KTL):
                    if kt >= 2:
                        is_turned(pool, "k", kt - 2)
                    k = keys_of(kt).rearrange("p (g d) -> p g d", d=HD)
                    nc.gpsimd.tensor_copy(khl[:, kt % 2, :, 0:HD].bitcast(F32R), k)
                    pool.drain()
                    nc.gpsimd.tensor_tensor(khl[:, kt % 2, :, HD:P], k, khl[:, kt % 2, :, 0:HD], ALU.subtract).then_inc(k_split, 1)
                for t in range(NT):
                    pool.wait_ge(o_sum, t + 1)
                    if t >= 2:
                        pool.wait_ge(o_ss, t - 1)
                    nc.gpsimd.tensor_tensor(osq[:, t % 2], of[:, t], of[:, t], ALU.mult).then_inc(o_sq, 1)
                pool.wait_ge(o_ss, NT)
                nc.gpsimd.tensor_scalar(oss[:], oss[:], 1.0 / HD, EPS, ALU.mult, ALU.add)
                pool.drain()
                nc.gpsimd.tensor_tensor(oss[:], oss[:], m["mhalf"][:, 0:36].rearrange("p (t h) -> p t h", h=4),
                                        ALU.pow).then_inc(o_root, 1)
                for n, (u, i) in enumerate(ASKS):
                    t0, _, _, _, g = UNITS[u]
                    if n >= 2:
                        is_turned(pool, "hi", *ASKS[n - 2])
                        is_turned(pool, "lo", *ASKS[n - 2])
                    q = z[:, t0 + i, 256 * g:256 * g + 256].rearrange("p (h d) -> p h d", d=HD)
                    for e in range(2):
                        nc.gpsimd.tensor_copy(qhh[:, n % 2, :, HD * e:HD * e + HD].bitcast(F32R), q)
                    pool.drain()
                    nc.gpsimd.tensor_tensor(ql[:, n % 2, :, 0:HD], q, qhh[:, n % 2, :, 0:HD], ALU.subtract).then_inc(q_split, 1)

            @block.scalar
            def _(act):
                act.wait_ge(ones_done, 1)
                for kt in range(KTL):
                    is_turned(act, "k", kt)
                    src = ps[:, 7, 0:256].rearrange("p (g c) -> p g c", c=P)
                    nc.scalar.activation(KH[:, :, kt * P:kt * P + P], src, ACT.Copy)
                    nc.scalar.activation(KO[0:HD, :, kt * P:kt * P + P], src[0:HD], ACT.Copy).then_inc(turn_copied, 1)
                for t in range(NT):
                    is_turned(act, "o", t)
                    nc.scalar.activation(br[:, 4:6, t * P:t * P + P], ps[:, 7, 0:256].rearrange("p (b c) -> p b c", c=P),
                                         ACT.Copy).then_inc(turn_copied, 1)

                def hi(u, i):
                    is_turned(act, "hi", u, i)
                    nc.scalar.activation(QH[:, u % 2, :, P * i:P * i + P], ps[:, 7, :].rearrange("p (h c) -> p h c", c=P),
                                         ACT.Copy).then_inc(turn_copied, 1)

                def lo(u, i):
                    is_turned(act, "lo", u, i)
                    nc.scalar.activation(QL[0:HD + 1, u % 2, :, P * i:P * i + P],
                                         ps[0:HD + 1, 7, :].rearrange("p (h c) -> p h c", c=P), ACT.Copy).then_inc(turn_copied, 1)

                def step(u, h, kt):
                    n, w = st_before[u, h, kt], P * UNITS[u][1]
                    act.wait_ge(st_done, n + 1)
                    if n >= 3:
                        act.wait_ge(pv_done, n - 2)
                    nc.scalar.activation(pr[:, n % 3, 0:w], ps[:, n % 3, 0:w], ACT.Exp, scale=HD ** -0.5).then_inc(p_done, 1)

                attention_order(hi, none, lo, none, step, none)

            @block.tensor
            def _(pe):
                def turn_start(*what):
                    if turn[what] >= 1:
                        pe.wait_ge(turn_copied, turn[what])

                for kt in range(KTL):
                    turn_start("k", kt)
                    pe.wait_ge(k_split, kt + 1)
                    for g in range(NKV):
                        last = nc.tensor.transpose(ps[:, 7, P * g:P * g + P], khl[:, kt % 2, g, :], m["ident"])
                    last.then_inc(turned, 1)
                for t in range(NT):
                    turn_start("o", t)
                    pe.wait_ge(o_ready, t + 1)
                    for b in range(2):
                        last = nc.tensor.transpose(ps[:, 7, P * b:P * b + P], of[:, t, P * b:P * b + P], m["ident"])
                    last.then_inc(turned, 1)

                def hi(u, i):
                    turn_start("hi", u, i)
                    n = ASKS.index((u, i))
                    pe.wait_ge(q_split, n + 1)
                    for h in range(Q_PER_KV):
                        last = nc.tensor.transpose(ps[:, 7, P * h:P * h + P], qhh[:, n % 2, h, :], m["ident"])
                    last.then_inc(turned, 1)

                def maxima(u, i, h):
                    g = UNITS[u][4]
                    is_turn_copied(pe, "hi", u, i)
                    for c, (k0, w) in enumerate(chunks(u)):
                        n = mx_before[u, i, h] + c
                        if n >= 2:
                            pe.wait_ge(mx_read, n - 1)
                        nc.tensor.matmul(ps[:, 5 + n % 2, 0:w], QH[:, u % 2, h, P * i:P * i + P], KH[:, g, k0:k0 + w],
                                         start=True, stop=True).then_inc(mx_product, 1)

                def lo(u, i):
                    turn_start("lo", u, i)
                    n = ASKS.index((u, i))
                    pe.wait_ge(m_done, n + 1)
                    for h in range(Q_PER_KV):
                        last = nc.tensor.transpose(ps[0:HD + 1, 7, P * h:P * h + P], ql[:, n % 2, h, 0:HD + 1], m["ident"])
                    last.then_inc(turned, 1)

                def scores(n):
                    u, h, kt = steps[n]
                    _, tiles, k0, _, g = UNITS[u]
                    if n >= 3:
                        pe.wait_ge(p_done, n - 2)
                    if h == 0 and kt == 0:
                        is_turn_copied(pe, "lo", u, tiles - 1)
                    ks, w = slice((k0 + kt) * P, (k0 + kt) * P + P), P * tiles
                    nc.tensor.matmul(ps[:, n % 3, 0:w], KH[:, g, ks], QH[:, u % 2, h, 0:w], start=True, stop=False)
                    nc.tensor.matmul(ps[:, n % 3, 0:w], KO[0:HD + 1, g, ks], QL[0:HD + 1, u % 2, h, 0:w],
                                     start=False, stop=True).then_inc(st_done, 1)

                def first(u, h):
                    if h == 0:
                        scores(st_before[u, 0, 0])

                def step(u, h, kt):
                    _, tiles, k0, keys, g = UNITS[u]
                    n, hn, w = st_before[u, h, kt], Q_PER_KV * u + h, P * tiles
                    if (h, kt) != (Q_PER_KV - 1, keys - 1):
                        scores(n + 1)
                    if kt == 0 and hn >= 2:
                        pe.wait_ge(o_done, hn - 1)
                    if n == 0:
                        pe.wait_ge(v_done, 1)
                    pe.wait_ge(p_done, n + 1)
                    nc.tensor.matmul(ps[:, 3 + hn % 2, 0:w], V[:, k0 + kt, g, :], pr[:, n % 3, 0:w],
                                     start=(kt == 0), stop=(kt == keys - 1)).then_inc(pv_done, 1)

                attention_order(hi, maxima, lo, first, step, none)

            @block.vector
            def _(dve):
                for t in range(NT):
                    nc.vector.tensor_tensor(of[:, t], of[:, t], ob[:, t], ALU.add).then_inc(o_sum, 1)
                dve.wait_ge(ones_done, 1)
                dve.wait_ge(cache_in, 32)
                for kt in range(KTL):
                    v = cvv[:] if kt == KTL - 2 else z[:, CTX if kt == KTL - 1 else kt, 640:768]
                    last = nc.vector.tensor_copy(V[:, kt, :, 0:HD], v.rearrange("p (g d) -> p g d", d=HD))
                last.then_inc(v_done, 1)
                for t in range(NT):
                    dve.wait_ge(o_sq, t + 1)
                    nc.vector.tensor_reduce(oss[:, t], osq[:, t % 2].rearrange("p (h d) -> p h d", d=HD), AX_X,
                                            ALU.add).then_inc(o_ss, 1)
                dve.wait_ge(o_root, 1)
                for t in range(NT):
                    o = of[:, t].rearrange("p (h d) -> p h d", d=HD)
                    nc.vector.tensor_tensor(o, o, oss[:, t].unsqueeze(2).broadcast_to([P, 4, HD]), ALU.mult)
                dve.drain()
                for t in range(NT):
                    o = of[:, t].rearrange("p (h d) -> p h d", d=HD)
                    nc.vector.tensor_tensor(o, o, m["on"].unsqueeze(1).broadcast_to([P, 4, HD]), ALU.mult).then_inc(o_ready, 1)

                def maxima(u, i, h):
                    ch, n = chunks(u), ASKS.index((u, i))
                    for c, (_, w) in enumerate(ch):
                        dve.wait_ge(mx_product, mx_before[u, i, h] + c + 1)
                        nc.vector.tensor_reduce(m3[:, n % 2, h, c:c + 1], ps[:, 5 + (mx_before[u, i, h] + c) % 2, 0:w],
                                                AX_X, ALU.max).then_inc(mx_read, 1)
                    if h == Q_PER_KV - 1:
                        dve.drain()
                        nc.vector.tensor_reduce(mx[:, n % 2], m3[:, n % 2, :, 0:len(ch)], AX_X, ALU.max)
                        dve.drain()
                        dve.wait_ge(q_split, n + 1)
                        nc.vector.tensor_scalar(ql[:, n % 2, :, HD], mx[:, n % 2], -1.0, None, ALU.mult).then_inc(m_done, 1)

                def last_of(u, h):
                    t0, tiles, _, keys, g = UNITS[u]
                    hn, w = Q_PER_KV * u + h, P * tiles
                    dve.wait_ge(pv_done, st_before[u, h, keys - 1] + 1)
                    acc = ps[:, 3 + hn % 2, 0:w]
                    nc.vector.reciprocal(rc[HD:P, hn % 2, 0:w], acc[HD:P])
                    dve.drain()
                    head = Q_PER_KV * g + h
                    half = slice(HD * (head % 2), HD * (head % 2) + HD)
                    nc.vector.tensor_tensor(br[half, head // 2, P * t0:P * t0 + w], acc[0:HD], rc[HD:P, hn % 2, 0:w],
                                            ALU.mult).then_inc(o_done, 1)

                attention_order(none, maxima, none, none, none, last_of)
        clear(nc, sem)


OUT_BLOCKS = [2, 3, 4, 5, 6, 7, 0, 1]


def project_out(nc, io, m, l):
    with ExitStack() as ctx:
        sem = Sems(nc, ctx, "out")

        def sb(name, shape, dt=F32):
            return ctx.enter_context(nc.sbuf_tensor(f"out_{name}", shape, dt))

        b_hi = sb("b_hi", [P, KD, T], F32R)
        with nc.sbuf_tensor("out_w", [P, KD, D], F32) as wst:
            pass
        w_lo = sb("w_lo", [P, KD, D], F32R)
        w_hi = sb("w_hi", [P, KD, D], F32R)
        x, y1 = sb("x", [P, 2, D]), sb("y1", [P, D])
        ss, rs = sb("ss", [P, NT]), sb("rs", [P, NT])
        flat = m["z"][:].rearrange("p t c -> p (t c)")
        gt = flat[:, 0:3 * T].rearrange("p (n t) -> p n t", t=T)
        grow = flat[:, 3 * T:3 * T + 2 * D].rearrange("p (c d) -> p c d", d=D)
        y = [y1[:], flat[:, 3 * T + 2 * D:3 * T + 3 * D]]
        b_lo = m["b_lo"]
        g_in, x_in, y_out = ([sem(f"{n}{i}") for i in range(k)] for n, k in (("g_in", 3), ("x_in", 2), ("y_out", 2)))
        w_in, w_split, gated, high, low = sem("w_in"), sem("w_split"), sem("gated"), sem("high"), sem("low")
        diag_done, spread, grow_done = sem("diag_done"), sem("spread"), sem("grow_done")
        product, summed, root, scaled, added = (sem(n) for n in ("product", "summed", "root", "scaled", "added"))
        ps, br = m["ps"], m["zc"]
        w_dram = layer(io["w_out"], l)

        def branch(e):
            return br[:, e, 0:T] if e < 6 else m["pbr"][:, e - 6, :]

        with nc.Block() as block:
            @block.sync
            def _(sp):
                for k, e in enumerate(OUT_BLOCKS):
                    sp.dma_start(wst[:, k], w_dram[P * e:P * e + P, :]).then_inc(w_in, 16)
                    if k >= 3:
                        sp.wait_ge(low, k - 2)
                    sp.dma_start(gt[:, k % 3], io["gates"][e]).then_inc(g_in[k % 3], 16)
                sp.wait_ge(spread, 2)
                for t in range(NT):
                    if t >= 2:
                        sp.wait_ge(added, t - 1)
                    load_x(nc, io, sp, l, t, x[:, t % 2, :], x_in[t % 2])
                    if t >= 1:
                        sp.wait_ge(added, t)
                        sp.dma_start(layer(io["y"], l)[P * (t - 1):P * t, :], y[(t - 1) % 2]).then_inc(y_out[(t - 1) % 2], 16)
                sp.wait_ge(added, NT)
                sp.dma_start(layer(io["y"], l)[P * (NT - 1):P * NT, :], y[(NT - 1) % 2]).then_inc(y_out[(NT - 1) % 2], 16)
                for i in range(2):
                    sp.wait_ge(y_out[i], 16 * ((NT + 1 - i) // 2))

            @block.scalar
            def _(act):
                for k in range(KD):
                    act.wait_ge(gated, k + 1)
                    nc.scalar.activation(b_hi[:, k, :], gt[:, k % 3], ACT.Copy).then_inc(high, 1)
                for c in range(2):
                    act.wait_ge(spread, c + 1)
                    for i in range(2):
                        last = nc.scalar.activation(grow[:, c, 512 * i:512 * i + 512], ps[:, 6 + i, :], ACT.Copy)
                    last.then_inc(grow_done, 1)
                for t in range(NT):
                    act.wait_ge(product, t + 1)
                    if t >= 2:
                        act.wait_ge(y_out[t % 2], 16 * (t // 2))
                    nc.scalar.activation(y[t % 2], ps[:, 2 * (t % 2):2 * (t % 2) + 2, :].rearrange("p b n -> p (b n)"),
                                         ACT.Square, accum_out=ss[:, t:t + 1]).then_inc(summed, 1)

            @block.gpsimd
            def _(pool):
                for c in range(2):
                    for k in range(KD):
                        if c == 1:
                            pool.wait_ge(spread, 1)
                        last = nc.gpsimd.tensor_scalar(x[:, 0, P * k:P * k + P] if c == 0 else x[:, 1, P * k:P * k + P],
                                                       m["ident"], m["gcol"][:, k, c:c + 1], None, ALU.mult)
                    last.then_inc(diag_done, 1)
                for k in range(KD):
                    pool.wait_ge(high, k + 1)
                    nc.gpsimd.tensor_tensor(b_lo[:, k, :], gt[:, k % 3], b_hi[:, k, :].bitcast(F32), ALU.subtract).then_inc(low, 1)
                for t in range(NT):
                    pool.wait_ge(summed, t + 1)
                    nc.gpsimd.tensor_scalar(rs[:, t:t + 1], ss[:, t:t + 1], 1.0 / D, EPS, ALU.mult, ALU.add)
                    pool.drain()
                    nc.gpsimd.tensor_tensor(rs[:, t:t + 1], rs[:, t:t + 1], m["mhalf"][:, 0:1], ALU.pow).then_inc(root, 1)
                    pool.wait_ge(scaled, t + 1)
                    pool.wait_ge(x_in[t % 2], 16 * (t // 2 + 1))
                    nc.gpsimd.tensor_tensor(y[t % 2], y[t % 2], x[:, t % 2, :], ALU.add).then_inc(added, 1)

            @block.vector
            def _(dve):
                for k in range(KD):
                    dve.wait_ge(g_in[k % 3], 16 * (k // 3 + 1))
                    nc.vector.tensor_tensor(gt[:, k % 3], gt[:, k % 3], branch(k), ALU.mult).then_inc(gated, 1)
                for k in range(KD):
                    dve.wait_ge(w_in, 16 * KD)
                    nc.vector.tensor_copy(w_hi[:, k], wst[:, k])
                dve.drain()
                for k in range(KD):
                    nc.vector.tensor_tensor(w_lo[:, k], wst[:, k], w_hi[:, k].bitcast(F32), ALU.subtract).then_inc(w_split, 1)
                dve.wait_ge(grow_done, 2)
                for t in range(NT):
                    dve.wait_ge(root, t + 1)
                    c = 1 if t == CTX else 0
                    nc.vector.scalar_tensor_tensor(out=y[t % 2], in0=ps[:, 2 * (t % 2):2 * (t % 2) + 2, :].rearrange("p b n -> p (b n)"),
                                                   scalar=rs[:, t:t + 1], in1=grow[:, c, :], op0=ALU.mult,
                                                   op1=ALU.mult).then_inc(scaled, 1)

            @block.tensor
            def _(pe):
                for c in range(2):
                    pe.wait_ge(diag_done, c + 1)
                    if c == 1:
                        pe.wait_ge(grow_done, 1)
                    for k in range(KD):
                        last = nc.tensor.matmul(ps[:, 6 + k // 4, P * (k % 4):P * (k % 4) + P], m["ones"],
                                                x[:, c, P * k:P * k + P], start=True, stop=True)
                    last.then_inc(spread, 1)
                pe.wait_ge(low, KD)
                pe.wait_ge(w_split, KD)
                for t in range(NT):
                    if t >= 2:
                        pe.wait_ge(scaled, t - 1)
                    tk = slice(P * t, P * t + P)
                    for i in range(2):
                        n = slice(512 * i, 512 * i + 512)
                        last = split3(nc, ps[:, 2 * (t % 2) + i, :], lambda k: b_hi[:, k, tk], lambda k: b_lo[:, k, tk],
                                      lambda k: w_hi[:, k, n], lambda k: w_lo[:, k, n], KD)
                    last.then_inc(product, 1)
        clear(nc, sem)


def build(nc, io):
    with ExitStack() as ctx:
        def sb(name, shape, dt=F32):
            return ctx.enter_context(nc.sbuf_tensor(name, shape, dt))

        m = {}
        masks = m["masks"] = sb("masks", [P, N_MASK, P])
        m["ident"] = masks[:, M_ID, :]
        m["mhalf"] = sb("mhalf", [P, 96])
        m["ps"] = ctx.enter_context(nc.psum_tensor("ps", [P, 8, 512], F32))
        for name, shape in (("poolw", [P, 2, P]), ("cols", [P, 66]), ("rows", [P, 208]), ("ea", [P, 8]), ("shift", [P, KD, 2]),
                            ("scale", [P, KD, 2]), ("gcol", [P, KD, 2]), ("beta", [P, NT, 8]), ("g", [P, NT, 8]),
                            ("gc", [P, NT, 8]), ("eg", [P, NT, 8]), ("ekd", [P, NT, 8]), ("beg", [P, NT, 8]),
                            ("egl", [P, 2, NT, 2, 2]), ("ones", [P, P]), ("ba", [16, T])):
            m[name] = sb(name, shape)
        m["ones"] = m["ones"][:]
        cols, rows = m["cols"], m["rows"]
        m["b_mod"], m["npre"], m["npost"], m["psc"] = cols[:, 0:24], cols[:, 24:32], cols[:, 32:40], cols[:, 40:42]
        m["convw"] = cols[:, 42:66].rearrange("p (j b) -> p j b", b=6)
        m["qn"], m["kn"], m["on"] = rows[:, 0:64], rows[:, 64:128], rows[:, 128:192]
        m["alog"], m["dtb"] = rows[:, 192:200], rows[:, 200:208]
        m["z"] = sb("z", [P, NT, QKV])
        zw = 6 * CW + 2 * UW
        with nc.sbuf_tensor("zz", [P, zw], F32) as zz:
            pass
        b_lo = sb("b_lo", [P, zw], F32R)
        m["b_lo"] = b_lo[:, 0:KD * T].rearrange("p (k t) -> p k t", t=T)
        m["zc"] = zz[:, 0:6 * CW].rearrange("p (b c) -> p b c", c=CW)
        m["zu"] = zz[:, 6 * CW:zw].rearrange("p (b c) -> p b c", c=UW)
        m["ob"] = zz[:, 6 * CW:6 * CW + NT * 256].rearrange("p (t c) -> p t c", c=256)
        const_in = ctx.enter_context(nc.semaphore("const_in"))
        with nc.Block() as block:
            @block.sync
            def _(sp):
                sp.dma_start(masks[:], io["masks"]).then_inc(const_in, 16)
                sp.wait_ge(const_in, 16)

            @block.vector
            def _(dve):
                nc.vector.memset(m["mhalf"][:], -0.5)
                nc.vector.memset(m["ones"], 1.0)
        with nc.Fori(0, DEPTH) as l:
            modulation(nc, io, m, l)
            with ExitStack() as part:
                m["h_hi"] = part.enter_context(nc.sbuf_tensor("h_hi", [P, KD, T], F32R))
                m["h_lo"] = part.enter_context(nc.sbuf_tensor("h_lo", [P, KD, T], F32R))
                normalise(nc, io, m, l)
                project_in(nc, io, m, l)
            with ExitStack() as part:
                m["pbr"] = part.enter_context(nc.sbuf_tensor("pbr", [P, 2, T], F32))
                with nc.sbuf_tensor("of", [P, NT, 256], F32) as of:
                    m["of"] = of
                    with nc.sbuf_tensor("tok", [P, NT, QKV], F32) as tok:
                        m["tok"] = tok
                        prepare_tokens(nc, io, m, l)
                        delta_rule(nc, io, m, l)
                    attention(nc, io, m, l)
                project_out(nc, io, m, l)


def shape_constants():
    import numpy as np
    j, i = np.arange(P)[:, None], np.arange(P)[None, :]
    same = j // 64 == i // 64
    masks = [j == i, same & (j <= i), same & (j >= i), same & (j < i), same & (j > i)]
    for d in range(2):
        for n in range(LEVELS):
            s = 2 ** n
            a, b = (j, i) if d == 0 else (i, j)
            masks.append((a // (2 * s) == b // (2 * s)) & (a % (2 * s) < s) & (b % (2 * s) >= s))
    masks += [(j < 64) & (i >= 0), (j >= 64) & (i >= 0), (j % 32 == i) & (i < 2)]
    masks = np.stack(masks, axis=1).astype(np.float32)
    tok = np.arange(N_LAT)
    inv = (10000.0 ** (-np.arange(0, 32, 2) / 32)).astype(np.float32)
    ang = np.concatenate([(tok // 64).astype(np.float32)[:, None] * inv, (tok % 64).astype(np.float32)[:, None] * inv], 1)
    cos, sin = np.repeat(np.cos(ang), 2, 1), np.repeat(np.sin(ang), 2, 1)
    sin[:, 0::2] *= -1
    rope = np.stack([cos, sin]).reshape(2, 8, P, HD).transpose(2, 0, 1, 3)
    inv_count = np.zeros((P, 2, T), np.float32)
    for g, w in enumerate(WINDOWS):
        for t0, n in SEQS:
            t = np.arange(n)
            c = np.clip(t - w // 2 + w, 0, n) - np.clip(t - w // 2, 0, n)
            inv_count[64 * (g % 2):64 * (g % 2) + 64, g // 2, t0:t0 + n] = 1.0 / c
    return {"masks": masks, "rope": np.ascontiguousarray(rope, np.float32), "inv_count": inv_count}


def kernel(x_prompt, x_sample, cache_attn_k, cache_attn_v, state_delta, c, c_ctx, w_mod, b_mod, norm_pre, norm_post,
           w_in, w_out, pool_w, pool_scale, q_norm, k_norm, conv_w, a_log, dt_bias, o_norm):
    import numpy as np
    import concourse.bacc as bacc
    from concourse.bass_utils import run_bass_kernel_spmd

    a = np.asarray

    def by_channel(x):
        return a(x).reshape(DEPTH, -1, P).transpose(0, 2, 1)

    conv = a(conv_w).reshape(DEPTH, 4 * 6, P).transpose(0, 2, 1)
    arrays = {
        "x_prompt": a(x_prompt), "x_sample": a(x_sample),
        "cond": np.stack([a(c).reshape(KD, P).T, a(c_ctx).reshape(KD, P).T], axis=2),
        "cache_k": a(cache_attn_k).reshape(DEPTH, P, NKV * HD), "cache_v": a(cache_attn_v).reshape(DEPTH, P, NKV * HD),
        "state_delta": a(state_delta).reshape(DEPTH, 2 * NDH * HD, HD), "w_mod": a(w_mod),
        "w_in": a(w_in), "w_out": a(w_out), "pool_w": a(pool_w).reshape(DEPTH, 256, 64),
        "cols": np.concatenate([by_channel(b_mod), by_channel(norm_pre), by_channel(norm_post), by_channel(pool_scale),
                                conv], axis=2),
        "rows": np.concatenate([a(q_norm), a(k_norm), a(o_norm), a(a_log).reshape(DEPTH, 8),
                                a(dt_bias).reshape(DEPTH, 8)], axis=1),
        **shape_constants()}
    nc = bacc.Bacc("TRN2", target_bir_lowering=False, num_devices=1)
    io = {n: nc.dram_tensor(f"in_{n}", v.shape, mybir.dt.from_np(v.dtype), kind="ExternalInput").ap() for n, v in arrays.items()}
    outs = {"y": (DEPTH, T, D), "new_k": (DEPTH, P, NKV * HD), "new_v": (DEPTH, P, NKV * HD),
            "new_state": (DEPTH, 2 * NDH * HD, HD)}
    for n, shape in outs.items():
        io[n] = nc.dram_tensor(f"out_{n}", shape, F32, kind="ExternalOutput").ap()
    io["gates"] = nc.dram_tensor("gates", (KD, P, T), F32, kind="Internal").ap()
    build(nc, io)
    r = run_bass_kernel_spmd(nc, [{f"in_{n}": np.ascontiguousarray(v) for n, v in arrays.items()}], core_ids=[0]).results[0]
    y = r["out_y"][DEPTH - 1]
    return (y[N_LAT:].reshape(1, N_CTX, D), y[:N_LAT].reshape(1, N_LAT, D),
            r["out_new_k"].reshape(1, DEPTH, P, NKV, HD), r["out_new_v"].reshape(1, DEPTH, P, NKV, HD),
            r["out_new_state"].reshape(1, DEPTH, 2, NDH, HD, HD))
```
